# Optimizing a Trainium2 kernel written in Bass

```python
import math
import jax, jax.numpy as jnp
from jax import lax
import numpy as np

D_MODEL = 1024
BATCH = 1
SEQ = 512
DEPTH = 1

HG_HEADS = 4
HG_KDIM = 128
HG_VDIM = 128
HG_KWIDTH = HG_HEADS * HG_KDIM
HG_WIDTH = HG_HEADS * HG_VDIM
DA_HEADS = 4
DA_HEAD_DIM = 64
DA_WIDTH = DA_HEADS * 2 * DA_HEAD_DIM
MIX_WIDTH = HG_WIDTH + DA_WIDTH
IN_SIZES = (HG_KWIDTH, HG_KWIDTH, HG_WIDTH, HG_WIDTH, DA_WIDTH, DA_WIDTH, DA_WIDTH)
IN_WIDTH = sum(IN_SIZES)
D_FF = -(-8 * D_MODEL // (3 * 256)) * 256
CHUNK = 64
Q_BLOCK = 128
EPS = 1e-6
N_MOD = 6


def rmsnorm(x, w):
    x32 = x.astype(jnp.float32)
    y = x32 * lax.rsqrt(jnp.mean(x32 * x32, axis=-1, keepdims=True) + EPS)
    return (y * w.astype(jnp.float32)).astype(x.dtype)

def alibi_slopes(n):
    return jnp.asarray(np.array([2.0 ** (-8.0 * (h + 1) / n) for h in range(n)], dtype=np.float32))

def hgrn2(q, f_logit, i, g, lb, gnorm_w):
    B, T, _ = q.shape
    n = T // CHUNK
    f = lb + (1.0 - lb) * jax.nn.sigmoid(f_logit.astype(jnp.float32))
    logf = jnp.log(f)
    k = 1.0 - f

    def heads(t, d):
        return t.reshape(B, n, CHUNK, HG_HEADS, d).transpose(1, 0, 3, 2, 4)

    qc = heads(q.astype(jnp.float32), HG_KDIM)
    kc = heads(k, HG_KDIM)
    vc = heads(i.astype(jnp.float32), HG_VDIM)
    bc = jnp.cumsum(heads(logf, HG_KDIM), axis=3)
    causal = jnp.tril(jnp.ones((CHUNK, CHUNK), dtype=bool))[:, :, None]

    def step(S, inp):
        qb, kb, vb, bb = inp
        o_inter = jnp.einsum('bhtk,bhkv->bhtv', qb * jnp.exp(bb), S)
        rel = bb[:, :, :, None, :] - bb[:, :, None, :, :]
        decay = jnp.exp(jnp.where(causal, rel, -jnp.inf))
        A = jnp.einsum('bhtk,bhsk,bhtsk->bhts', qb, kb, decay)
        o = o_inter + jnp.einsum('bhts,bhsv->bhtv', A, vb)
        blast = bb[:, :, -1:, :]
        S_new = jnp.exp(blast[:, :, 0, :])[..., None] * S + jnp.einsum('bhsk,bhsv->bhkv', kb * jnp.exp(blast - bb), vb)
        return S_new, o

    S0 = jnp.zeros((B, HG_HEADS, HG_KDIM, HG_VDIM), jnp.float32)
    _, o = lax.scan(step, S0, (qc, kc, vc, bc))
    o = o.transpose(1, 0, 3, 2, 4).reshape(B, T, HG_HEADS, HG_VDIM)
    o = rmsnorm(o, gnorm_w) * jax.nn.silu(g.reshape(B, T, HG_HEADS, HG_VDIM).astype(jnp.float32))
    return o.reshape(B, T, HG_WIDTH).astype(q.dtype)

def diff_attention(q, k, v, lam, lambda_init, subln_w):
    B, T, _ = q.shape
    d = DA_HEAD_DIM
    q = q.reshape(B, T, DA_HEADS, 2, d).transpose(0, 2, 3, 1, 4)
    k = k.reshape(B, T, DA_HEADS, 2, d).transpose(0, 2, 3, 1, 4)
    v = v.reshape(B, T, DA_HEADS, 2 * d).transpose(0, 2, 1, 3)
    scale = d ** -0.5
    slopes = alibi_slopes(DA_HEADS)
    pos = jnp.arange(T)
    outs = []
    for blk in range(T // Q_BLOCK):
        lo, hi = blk * Q_BLOCK, (blk + 1) * Q_BLOCK
        qb, kb, vb = q[:, :, :, lo:hi], k[:, :, :, :hi], v[:, :, :hi]
        s = jnp.einsum('bhmqd,bhmkd->bhmqk', qb, kb).astype(jnp.float32) * scale
        dist = (pos[lo:hi, None] - pos[None, :hi]).astype(jnp.float32)
        s = s - (slopes[:, None, None] * dist)[None, :, None]
        s = jnp.where(dist >= 0, s, -jnp.inf)
        p = jax.nn.softmax(s, axis=-1)
        w = p[:, :, 0] - lam * p[:, :, 1]
        outs.append(jnp.einsum('bhqk,bhkv->bhqv', w.astype(v.dtype), vb))
    o = jnp.concatenate(outs, axis=2)
    o = rmsnorm(o, subln_w) * (1.0 - lambda_init)
    return o.transpose(0, 2, 1, 3).reshape(B, T, DA_WIDTH)

def first_inputs(seed: int = 0) -> dict:
    key = jax.random.key(seed)
    ks = jax.random.split(key, 20)
    f32 = jnp.float32
    nrm = lambda k, shape, s: jax.random.normal(k, shape, f32) * s
    return {
        "x": nrm(ks[0], (BATCH, SEQ, D_MODEL), 1.0),
        "c": nrm(ks[1], (BATCH, D_MODEL), 1.0),
        "w_ada": nrm(ks[2], (DEPTH, D_MODEL, N_MOD * D_MODEL), 0.5 * D_MODEL ** -0.5),
        "b_ada": nrm(ks[3], (DEPTH, N_MOD * D_MODEL), 0.01),
        "norm1_w": 1.0 + nrm(ks[4], (DEPTH, D_MODEL), 0.02),
        "w_in": nrm(ks[5], (DEPTH, D_MODEL, IN_WIDTH), D_MODEL ** -0.5),
        "hgrn_lb_logits": nrm(ks[6], (DEPTH + 1, HG_KWIDTH), 0.5),
        "hgrn_gnorm_w": 1.0 + nrm(ks[7], (DEPTH, HG_VDIM), 0.02),
        "diff_lambda_q1": nrm(ks[8], (DEPTH, DA_HEAD_DIM), 0.1),
        "diff_lambda_k1": nrm(ks[9], (DEPTH, DA_HEAD_DIM), 0.1),
        "diff_lambda_q2": nrm(ks[10], (DEPTH, DA_HEAD_DIM), 0.1),
        "diff_lambda_k2": nrm(ks[11], (DEPTH, DA_HEAD_DIM), 0.1),
        "diff_subln_w": 1.0 + nrm(ks[12], (DEPTH, 2 * DA_HEAD_DIM), 0.02),
        "w_out": nrm(ks[13], (DEPTH, MIX_WIDTH, D_MODEL), MIX_WIDTH ** -0.5),
        "norm2_w": 1.0 + nrm(ks[14], (DEPTH, D_MODEL), 0.02),
        "w_ffn_gate": nrm(ks[15], (DEPTH, D_MODEL, D_FF), D_MODEL ** -0.5),
        "w_ffn_up": nrm(ks[16], (DEPTH, D_MODEL, D_FF), D_MODEL ** -0.5),
        "w_ffn_down": nrm(ks[17], (DEPTH, D_FF, D_MODEL), D_FF ** -0.5),
        "final_norm_w": 1.0 + nrm(ks[18], (D_MODEL,), 0.02),
    }

def first_block(x, c, w_ada, b_ada, norm1_w, w_in, hgrn_lb_logits, hgrn_gnorm_w,
              diff_lambda_q1, diff_lambda_k1, diff_lambda_q2, diff_lambda_k2, diff_subln_w,
              w_out, norm2_w, w_ffn_gate, w_ffn_up, w_ffn_down, final_norm_w):
    offs = np.cumsum(IN_SIZES)[:-1].tolist()
    lower_bounds = jnp.cumsum(jax.nn.softmax(hgrn_lb_logits.astype(jnp.float32), axis=0), axis=0)
    h = x
    for l in range(DEPTH):
        mod = jax.nn.silu(c) @ w_ada[l] + b_ada[l]
        sh1, sc1, g1, sh2, sc2, g2 = jnp.split(mod[:, None, :], N_MOD, axis=-1)
        u = rmsnorm(h, norm1_w[l]) * (1.0 + sc1) + sh1
        proj = u @ w_in[l]
        hq, hf, hi, hg, aq, ak, av = jnp.split(proj, offs, axis=-1)
        o_hg = hgrn2(hq, hf, hi, hg, lower_bounds[l], hgrn_gnorm_w[l])
        lambda_init = 0.8 - 0.6 * math.exp(-0.3 * l)
        lam = (jnp.exp(jnp.sum(diff_lambda_q1[l].astype(jnp.float32) * diff_lambda_k1[l].astype(jnp.float32)))
               - jnp.exp(jnp.sum(diff_lambda_q2[l].astype(jnp.float32) * diff_lambda_k2[l].astype(jnp.float32)))
               + lambda_init)
        o_da = diff_attention(aq, ak, av, lam, lambda_init, diff_subln_w[l])
        mix = jnp.concatenate([o_hg, o_da.astype(o_hg.dtype)], axis=-1) @ w_out[l]
        h = h + g1 * mix
        u = rmsnorm(h, norm2_w[l]) * (1.0 + sc2) + sh2
        ff = (jax.nn.silu(u @ w_ffn_gate[l]) * (u @ w_ffn_up[l])) @ w_ffn_down[l]
        h = h + g2 * ff
    return rmsnorm(h, final_norm_w)


HEAD_DIM = 64
NSA_HEADS = 8
NSA_KV_GROUPS = 2
NSA_REP = NSA_HEADS // NSA_KV_GROUPS
SB_HEADS = 8
CMP_BLOCK = 32
CMP_STRIDE = 16
CMP_HIDDEN = 2 * HEAD_DIM
SEL_BLOCK = 64
SEL_TOPK = 8
WINDOW = 512
SEL_Q_CHUNK = 64
D_FF_2 = -(-8 * D_MODEL // (3 * 256)) * 256
RMS_EPS = 1e-6
NEG_INF = -1e30
FORCE_PRIORITY = 1e4
ATTN_SCALE = 1.0 / math.sqrt(HEAD_DIM)

NSA_Q_DIM = NSA_HEADS * HEAD_DIM
NSA_KV_DIM = 6 * NSA_KV_GROUPS * HEAD_DIM
NSA_GATE_DIM = 3 * NSA_HEADS
SB_QKV_DIM = 3 * SB_HEADS * HEAD_DIM
MERGE_DIM = 2 * D_MODEL
D_IN = NSA_Q_DIM + NSA_KV_DIM + NSA_GATE_DIM + SB_QKV_DIM + MERGE_DIM
IN_SPLITS = (NSA_Q_DIM, NSA_Q_DIM + NSA_KV_DIM, NSA_Q_DIM + NSA_KV_DIM + NSA_GATE_DIM,
             NSA_Q_DIM + NSA_KV_DIM + NSA_GATE_DIM + SB_QKV_DIM)


def rmsnorm_2(x, g):
    xf = x.astype(jnp.float32)
    y = xf * lax.rsqrt(jnp.mean(xf * xf, axis=-1, keepdims=True) + RMS_EPS)
    return (y * g.astype(jnp.float32)).astype(x.dtype)

def modulate(h, shift, scale):
    return h * (1.0 + scale) + shift

def alibi_slopes_2():
    i = jnp.arange(1, NSA_HEADS + 1, dtype=jnp.float32)
    return jnp.exp2(-8.0 * i / NSA_HEADS).reshape(NSA_KV_GROUPS, NSA_REP)

def compress(k, pos_emb, w1, w2):
    n_cmp = (k.shape[2] - CMP_BLOCK) // CMP_STRIDE + 1
    idx = jnp.arange(n_cmp)[:, None] * CMP_STRIDE + jnp.arange(CMP_BLOCK)[None, :]
    blocks = k[:, :, idx] + pos_emb
    flat = blocks.reshape(*blocks.shape[:3], CMP_BLOCK * HEAD_DIM)
    return jax.nn.gelu(flat @ w1) @ w2

def nsa_compressed(q, kc, vc, slopes):
    S = q.shape[3]
    n = kc.shape[2]
    t = jnp.arange(S)
    end = jnp.arange(n) * CMP_STRIDE + CMP_BLOCK - 1
    dist = (t[:, None] - end[None, :]).astype(jnp.float32)
    valid = dist >= 0
    s = jnp.einsum('bgrqd,bgnd->bgrqn', q.astype(jnp.float32), kc.astype(jnp.float32)) * ATTN_SCALE
    s = s - slopes[:, :, None, None] * dist
    s = jnp.where(valid, s, NEG_INF)
    p = jax.nn.softmax(s, axis=-1)
    p = jnp.where(valid.any(-1)[:, None], p, 0.0)
    o = jnp.einsum('bgrqn,bgnd->bgrqd', p.astype(vc.dtype), vc)
    return o, p.sum(axis=2)

def nsa_select_indices(p_cmp, S):
    n_cmp = p_cmp.shape[-1]
    n_sel = S // SEL_BLOCK
    c_start = jnp.arange(n_cmp) * CMP_STRIDE
    c_end = c_start + CMP_BLOCK - 1
    s_start = jnp.arange(n_sel) * SEL_BLOCK
    s_end = s_start + SEL_BLOCK - 1
    overlap = ((c_start[:, None] <= s_end[None, :]) & (c_end[:, None] >= s_start[None, :])).astype(jnp.float32)
    p_slc = jnp.einsum('bgqn,nj->bgqj', p_cmp, overlap)
    cur = (jnp.arange(S) // SEL_BLOCK)[:, None]
    j = jnp.arange(n_sel)[None, :]
    valid = j <= cur
    forced = (j == 0) | (j == cur) | (j == cur - 1)
    prio = jnp.where(valid, p_slc, NEG_INF)
    prio = jnp.where(forced & valid, FORCE_PRIORITY, prio)
    _, idx = lax.top_k(prio, min(SEL_TOPK, n_sel))
    return idx

def nsa_selected(q, k, v, idx, slopes):
    B, G, R, S, hd = q.shape
    n = idx.shape[-1]
    kb = k.reshape(B, G, S // SEL_BLOCK, SEL_BLOCK, hd)
    vb = v.reshape(B, G, S // SEL_BLOCK, SEL_BLOCK, hd)
    nc = S // SEL_Q_CHUNK
    q_c = q.reshape(B, G, R, nc, SEL_Q_CHUNK, hd).transpose(3, 0, 1, 2, 4, 5)
    idx_c = idx.reshape(B, G, nc, SEL_Q_CHUNK, n).transpose(2, 0, 1, 3, 4)
    t_c = jnp.arange(S).reshape(nc, SEL_Q_CHUNK)
    bi = jnp.arange(B)[:, None, None, None]
    gi = jnp.arange(G)[None, :, None, None]

    def chunk(args):
        qq, ii, tt = args
        ks = kb[bi, gi, ii]
        vs = vb[bi, gi, ii]
        pos = ii[..., None] * SEL_BLOCK + jnp.arange(SEL_BLOCK)
        dist = (tt[:, None, None] - pos).astype(jnp.float32)
        s = jnp.einsum('bgrqd,bgqnld->bgrqnl', qq.astype(jnp.float32), ks.astype(jnp.float32)) * ATTN_SCALE
        s = s - slopes[:, :, None, None, None] * dist[:, :, None]
        s = jnp.where((dist >= 0)[:, :, None], s, NEG_INF)
        p = jax.nn.softmax(s, axis=(-2, -1))
        return jnp.einsum('bgrqnl,bgqnld->bgrqd', p.astype(v.dtype), vs)

    o = lax.map(chunk, (q_c, idx_c, t_c))
    return o.transpose(1, 2, 3, 0, 4, 5).reshape(B, G, R, S, hd)

def nsa_window(q, k, v, slopes):
    B, G, R, S, hd = q.shape
    kp = jnp.pad(k, ((0, 0), (0, 0), (WINDOW, 0), (0, 0)))
    vp = jnp.pad(v, ((0, 0), (0, 0), (WINDOW, 0), (0, 0)))
    nq = S // Q_BLOCK
    q_c = q.reshape(B, G, R, nq, Q_BLOCK, hd).transpose(3, 0, 1, 2, 4, 5)
    starts = jnp.arange(nq) * Q_BLOCK
    span = WINDOW + Q_BLOCK

    def blk(args):
        qq, q0 = args
        kk = lax.dynamic_slice_in_dim(kp, q0, span, axis=2)
        vv = lax.dynamic_slice_in_dim(vp, q0, span, axis=2)
        t = q0 + jnp.arange(Q_BLOCK)
        s_pos = q0 - WINDOW + jnp.arange(span)
        dist = t[:, None] - s_pos[None, :]
        mask = (dist >= 0) & (dist < WINDOW) & (s_pos[None, :] >= 0)
        s = jnp.einsum('bgrqd,bgkd->bgrqk', qq.astype(jnp.float32), kk.astype(jnp.float32)) * ATTN_SCALE
        s = s - slopes[:, :, None, None] * dist.astype(jnp.float32)
        s = jnp.where(mask, s, NEG_INF)
        p = jax.nn.softmax(s, axis=-1)
        return jnp.einsum('bgrqk,bgkd->bgrqd', p.astype(v.dtype), vv)

    o = lax.map(blk, (q_c, starts))
    return o.transpose(1, 2, 3, 0, 4, 5).reshape(B, G, R, S, hd)

def stick_breaking(q, k, v):
    B, H, S, hd = q.shape
    nq = S // Q_BLOCK
    q_c = q.reshape(B, H, nq, Q_BLOCK, hd).transpose(2, 0, 1, 3, 4)
    starts = jnp.arange(nq) * Q_BLOCK
    kf = k.astype(jnp.float32)
    s_pos = jnp.arange(S)

    def blk(args):
        qq, q0 = args
        t = q0 + jnp.arange(Q_BLOCK)
        mask = s_pos[None, :] < t[:, None]
        z = jnp.einsum('bhqd,bhkd->bhqk', qq.astype(jnp.float32), kf) * ATTN_SCALE
        log_keep = jnp.where(mask, -jax.nn.softplus(z), 0.0)
        later = lax.cumsum(log_keep, axis=3, reverse=True) - log_keep
        a = jnp.where(mask, jnp.exp(jax.nn.log_sigmoid(z) + later), 0.0)
        return jnp.einsum('bhqk,bhkd->bhqd', a.astype(v.dtype), v)

    o = lax.map(blk, (q_c, starts))
    return o.transpose(1, 2, 0, 3, 4).reshape(B, H, S, hd)

def hybrid_mixer(h, w_in, cmp_pos_k, cmp_w1_k, cmp_w2_k, cmp_pos_v, cmp_w1_v, cmp_w2_v,
                 w_proj_a, w_proj_b, w_out):
    B, S, _ = h.shape
    G, R, hd = NSA_KV_GROUPS, NSA_REP, HEAD_DIM
    proj = h @ w_in
    q_a, kv_a, gate_a, qkv_b, merge = jnp.split(proj, IN_SPLITS, axis=-1)

    q_a = q_a.reshape(B, S, G, R, hd).transpose(0, 2, 3, 1, 4)
    kv_a = kv_a.reshape(B, S, 6, G, hd).transpose(2, 0, 3, 1, 4)
    k_cmp, v_cmp, k_sel, v_sel, k_win, v_win = (kv_a[i] for i in range(6))
    g_a = jax.nn.sigmoid(gate_a.reshape(B, S, G, R, 3).transpose(0, 2, 3, 1, 4))
    slopes = alibi_slopes_2()
    kc = compress(k_cmp, cmp_pos_k, cmp_w1_k, cmp_w2_k)
    vc = compress(v_cmp, cmp_pos_v, cmp_w1_v, cmp_w2_v)
    o_cmp, p_cmp = nsa_compressed(q_a, kc, vc, slopes)
    idx = nsa_select_indices(p_cmp, S)
    o_sel = nsa_selected(q_a, k_sel, v_sel, idx, slopes)
    o_win = nsa_window(q_a, k_win, v_win, slopes)
    o_a = g_a[..., 0:1] * o_cmp + g_a[..., 1:2] * o_sel + g_a[..., 2:3] * o_win
    y_a = o_a.transpose(0, 3, 1, 2, 4).reshape(B, S, NSA_Q_DIM) @ w_proj_a

    qkv_b = qkv_b.reshape(B, S, 3, SB_HEADS, hd).transpose(2, 0, 3, 1, 4)
    o_b = stick_breaking(qkv_b[0], qkv_b[1], qkv_b[2])
    y_b = o_b.transpose(0, 2, 1, 3).reshape(B, S, SB_HEADS * hd) @ w_proj_b

    merge = merge.reshape(B, S, 2, D_MODEL)
    y = jax.nn.sigmoid(merge[:, :, 0]) * y_a + jax.nn.sigmoid(merge[:, :, 1]) * y_b
    return y @ w_out

def swiglu(h, w_gate, w_up, w_down):
    return (jax.nn.silu(h @ w_gate) * (h @ w_up)) @ w_down

def second_inputs(seed: int = 0) -> dict:
    key = jax.random.key(seed)
    ks = jax.random.split(key, 20)

    def dense(k, shape, fan_in):
        return jax.random.normal(k, shape, jnp.float32) * (fan_in ** -0.5)

    def gain(k, shape):
        return 1.0 + 0.05 * jax.random.normal(k, shape, jnp.float32)

    L = DEPTH
    cmp_in = CMP_BLOCK * HEAD_DIM
    return {
        "x": jax.random.normal(ks[0], (BATCH, SEQ, D_MODEL), jnp.float32),
        "c": jax.random.normal(ks[1], (BATCH, D_MODEL), jnp.float32),
        "w_ada": dense(ks[2], (L, D_MODEL, 6 * D_MODEL), D_MODEL),
        "b_ada": 0.02 * jax.random.normal(ks[3], (L, 6 * D_MODEL), jnp.float32),
        "norm_mix_g": gain(ks[4], (L, D_MODEL)),
        "w_in": dense(ks[5], (L, D_MODEL, D_IN), D_MODEL),
        "cmp_pos_k": 0.02 * jax.random.normal(ks[6], (L, CMP_BLOCK, HEAD_DIM), jnp.float32),
        "cmp_w1_k": dense(ks[7], (L, cmp_in, CMP_HIDDEN), cmp_in),
        "cmp_w2_k": dense(ks[8], (L, CMP_HIDDEN, HEAD_DIM), CMP_HIDDEN),
        "cmp_pos_v": 0.02 * jax.random.normal(ks[9], (L, CMP_BLOCK, HEAD_DIM), jnp.float32),
        "cmp_w1_v": dense(ks[10], (L, cmp_in, CMP_HIDDEN), cmp_in),
        "cmp_w2_v": dense(ks[11], (L, CMP_HIDDEN, HEAD_DIM), CMP_HIDDEN),
        "w_proj_a": dense(ks[12], (L, NSA_Q_DIM, D_MODEL), NSA_Q_DIM),
        "w_proj_b": dense(ks[13], (L, SB_HEADS * HEAD_DIM, D_MODEL), SB_HEADS * HEAD_DIM),
        "w_out": dense(ks[14], (L, D_MODEL, D_MODEL), D_MODEL),
        "norm_ffn_g": gain(ks[15], (L, D_MODEL)),
        "w_ffn_gate": dense(ks[16], (L, D_MODEL, D_FF_2), D_MODEL),
        "w_ffn_up": dense(ks[17], (L, D_MODEL, D_FF_2), D_MODEL),
        "w_ffn_down": dense(ks[18], (L, D_FF_2, D_MODEL), D_FF_2),
        "norm_final_g": gain(ks[19], (D_MODEL,)),
    }

def second_block(x, c, w_ada, b_ada, norm_mix_g, w_in, cmp_pos_k, cmp_w1_k, cmp_w2_k,
              cmp_pos_v, cmp_w1_v, cmp_w2_v, w_proj_a, w_proj_b, w_out, norm_ffn_g,
              w_ffn_gate, w_ffn_up, w_ffn_down, norm_final_g):
    for l in range(DEPTH):
        mod = jax.nn.silu(c) @ w_ada[l] + b_ada[l]
        sh1, sc1, g1, sh2, sc2, g2 = jnp.split(mod[:, None, :], 6, axis=-1)
        h = modulate(rmsnorm_2(x, norm_mix_g[l]), sh1, sc1)
        x = x + g1 * hybrid_mixer(h, w_in[l], cmp_pos_k[l], cmp_w1_k[l], cmp_w2_k[l],
                                  cmp_pos_v[l], cmp_w1_v[l], cmp_w2_v[l],
                                  w_proj_a[l], w_proj_b[l], w_out[l])
        h = modulate(rmsnorm_2(x, norm_ffn_g[l]), sh2, sc2)
        x = x + g2 * swiglu(h, w_ffn_gate[l], w_ffn_up[l], w_ffn_down[l])
    return rmsnorm_2(x, norm_final_g)


def setup_inputs(seed=0):
    out = dict(first_inputs(seed))
    for name, value in second_inputs(seed + 1).items():
        if name != "x":
            out[name + "_2"] = value
    return out


def reference(
    x, c, w_ada, b_ada, norm1_w, w_in, hgrn_lb_logits, hgrn_gnorm_w, diff_lambda_q1,
    diff_lambda_k1, diff_lambda_q2, diff_lambda_k2, diff_subln_w, w_out, norm2_w, w_ffn_gate,
    w_ffn_up, w_ffn_down, final_norm_w, c_2, w_ada_2, b_ada_2, norm_mix_g_2, w_in_2,
    cmp_pos_k_2, cmp_w1_k_2, cmp_w2_k_2, cmp_pos_v_2, cmp_w1_v_2, cmp_w2_v_2, w_proj_a_2,
    w_proj_b_2, w_out_2, norm_ffn_g_2, w_ffn_gate_2, w_ffn_up_2, w_ffn_down_2, norm_final_g_2,
):
    x = first_block(
        x, c, w_ada, b_ada, norm1_w, w_in, hgrn_lb_logits, hgrn_gnorm_w, diff_lambda_q1,
        diff_lambda_k1, diff_lambda_q2, diff_lambda_k2, diff_subln_w, w_out, norm2_w,
        w_ffn_gate, w_ffn_up, w_ffn_down, final_norm_w,
    )
    return second_block(
        x, c_2, w_ada_2, b_ada_2, norm_mix_g_2, w_in_2, cmp_pos_k_2, cmp_w1_k_2, cmp_w2_k_2,
        cmp_pos_v_2, cmp_w1_v_2, cmp_w2_v_2, w_proj_a_2, w_proj_b_2, w_out_2, norm_ffn_g_2,
        w_ffn_gate_2, w_ffn_up_2, w_ffn_down_2, norm_final_g_2,
    )


_drawn_inputs = setup_inputs


def setup_inputs(seed=0):
    import zlib

    import numpy as np

    out = dict(_drawn_inputs(seed))
    spreads = {}
    factors = {'b_ada': 4.121,
     'norm1_w': 7.383,
     'hgrn_gnorm_w': 8.0,
     'diff_lambda_q1': 4.001,
     'diff_lambda_k1': 64.0,
     'diff_lambda_q2': 64.0,
     'diff_subln_w': 64.0,
     'norm2_w': 8.0,
     'cmp_pos_k_2': 200.0,
     'cmp_pos_v_2': 23.843,
     'diff_lambda_k2': 8.0}
    for name, (base, spread) in spreads.items():
        noise = np.random.default_rng([zlib.crc32(name.encode()), seed]).standard_normal(out[name].shape)
        drawn = base * np.exp(spread * noise) if base else spread * noise
        out[name] = __import__('jax').numpy.asarray(drawn.astype(out[name].dtype))
    for name, factor in factors.items():
        out[name] = (out[name] * factor).astype(out[name].dtype)
    return out
```

```python
from contextlib import ExitStack

import concourse.bass as bass
from concourse import mybir

F32 = mybir.dt.float32
F32R = mybir.dt.float32r
I32 = mybir.dt.int32
ALU = mybir.AluOpType
ACT = mybir.ActivationFunctionType
AX_X = mybir.AxisListType.X
ds = bass.ds

P = 128
T = 512
NT = T // P
D = 1024
KT = D // P
F = 2816
FT = F // P
HEADS1 = 4
NSA_H, GROUPS, REP, HD = 8, 2, 4, 64
NCMP, CPAD, CSTRIDE, CBLOCK = 31, 32, 16, 32
EPS = 1e-6
BIG = -1.0e30
SCALE = HD ** -0.5
INV = 1.0 / SCALE
LAMBDA_INIT = 0.2
MODC = 256
LEVELS = [64, 32, 16, 8, 4, 2, 1]
ZOFF = [0, 128, 384, 768]
ZLEN = [P * (i + 1) for i in range(NT)]
ZW = sum(ZLEN)

CLAMP, SQ_SCALE, SQ_BACK, SQ_OVER = 2.0 ** 64, 2.0 ** -34, 2.0 ** 68, 2.0 ** 60

B_ADA, NORM_A, NORM_B, NORM_F, LB, GNORM, SUBLN = 0, 48, 56, 64, 72, 80, 81
POS_K, POS_V = 72, 88
U1, H1, Y1 = 1, 1, 1


class Phase:

    def __init__(self, name, iters, units, act, dve):
        self.name, self.iters, self.units, self.act, self.dve = name, iters, units, act, dve


def plan():
    order = [
        Phase("q1", 2, 2, 2, 0), Phase("f1", 2, 2, 2, 0), Phase("i1", 2, 2, 2, 0),
        Phase("g1", 2, 2, 2, 0), Phase("a1", 6, 2, 2, 0),
        Phase("out1", 4, 2, 0, 2), Phase("ff1", 22, 2, 1, 0), Phase("down1", 4, 6, 0, 2),
        Phase("qa2", 2, 2, 2, 0), Phase("kv2", 1, 7, 7, 0), Phase("b2", 6, 2, 2, 0),
        Phase("merge2", 8, 4, 2, 2),
        Phase("out2", 4, 2, 0, 2), Phase("ff2", 22, 2, 1, 0), Phase("down2", 4, 6, 0, 2),
    ]
    u, a, d = 0, KT, 2
    for ph in order:
        ph.u0, ph.a0, ph.d0 = u, a, d
        u, a, d = u + ph.iters * ph.units, a + ph.iters * ph.act, d + ph.iters * ph.dve
    return {ph.name: ph for ph in order}, u


def build(nc, t_in, out):
    PH, UNITS = plan()
    ctx = ExitStack()
    with ctx:
        base = 16640
        here = [base]

        def at(name, shape, dt=F32, where=None):
            n = 4
            for s in shape[1:]:
                n *= s
            off = here[0] if where is None else where
            if where is None:
                here[0] += (n + 31) // 32 * 32
            return nc.alloc_sbuf_tensor_at(name, shape, dt, offset=off)

        res = at("res", [P, KT, T])
        u_at = here[0]
        uh = at("uh", [P, KT, T], F32R)
        ul = at("ul", [P, KT, T], F32R)
        wraw = at("wraw", [P, 2, KT * P])
        wh = at("wh", [P, 2, KT * P], F32R)
        wl = at("wl", [P, 2, KT * P], F32R)
        a_at = here[0]
        ada = at("ada", [P, KT, MODC])
        acc = at("acc", [P, MODC])
        ident = at("ident", [P, P])
        ones = at("ones", [P, P])
        vt1 = at("vt1", [P, P])
        vt2 = at("vt2", [P, P])
        mod1 = at("mod1", [P, 48])
        mod2 = at("mod2", [P, 48])
        gain = at("gain", [P, 4, KT])
        sc_c = at("sc_c", [P, 2, KT])
        ct = at("ct", [P, 2, KT])
        lamv = at("lamv", [P, 4, HD])
        tiny = at("tiny", [P, 64])
        n_at = here[0]
        ssq = at("ssq", [P, T])
        sq = at("sq", [P, 2, T])
        rstd = at("rstd", [P, T])
        tn = at("tn", [P, 2, T])
        u32 = at("u32", [P, 2, T])
        r_at = here[0]
        K2 = 4 * T

        xin = at("xin", [P, NT, D], where=r_at)
        ada0 = at("ada0", [P, 8, KT, MODC], where=r_at + 8 * K2)
        v1 = at("v1", [P, P], where=r_at + 8 * K2 + 32 * K2)
        v2 = at("v2", [P, P], where=r_at + 8 * K2 + 32 * K2 + 512)
        p1 = at("p1", [P, 28, T], where=r_at)
        mixh = at("mixh", [P, KT, T], F32R, where=r_at + 28 * K2)
        mixl = at("mixl", [P, KT, T], F32R, where=r_at + 36 * K2)
        s_at = r_at + 44 * K2
        bb = at("bb", [P, T], where=u_at)
        xx = at("xx", [P, 2, T], where=u_at + 1 * K2)
        ql = at("ql", [P, 2, T], where=u_at + 3 * K2)
        kl = at("kl", [P, 2, T], where=u_at + 5 * K2)
        am = at("am", [P, T], where=u_at + 7 * K2)
        q0 = at("q0", [P, T], where=u_at + 8 * K2)
        kht = at("kht", [P, T], where=u_at + 9 * K2)
        vtm = at("vtm", [P, T], where=u_at + 10 * K2)
        st = at("st", [P, 3, P], where=u_at + 11 * K2)
        ff = at("ff", [P, T], where=u_at + 12 * K2)
        rmask = at("rmask", [P, T], where=u_at + 13 * K2)
        lmask = at("lmask", [P, 8, P], I32, where=n_at + 3 * K2)
        junk = at("junk", [P, T], where=u_at + 14 * K2)
        z1 = at("z1", [P, 2, ZW], where=s_at)
        dm1 = at("dm1", [P, T], where=n_at + 2 * K2 + K2 * 3)
        wt1 = at("wt1", [P, 2, NT, T], where=u_at)
        vd1 = at("vd1", [P, 2, T], where=u_at + 8 * K2)
        junk1 = at("junk1", [P, T], where=u_at + 10 * K2)
        clamped = at("clamped", [P, T], where=u_at + 11 * K2)
        hh = at("hh", [P, FT, T], F32R, where=r_at)
        hl = at("hl", [P, FT, T], F32R, where=r_at + FT * K2)
        sg = at("sg", [P, 2, T], where=r_at + 2 * FT * K2)
        hf = at("hf", [P, 2, T], where=r_at + 2 * FT * K2 + 2 * K2)
        qa = at("qa", [P, 4, T], where=r_at)
        kdup = at("kdup", [P, 2, GROUPS, T], where=r_at + 4 * K2)
        qkvb = at("qkvb", [P, 12, T], where=r_at + 8 * K2)
        vsw = at("vsw", [P, 2, T], where=r_at + 20 * K2)
        vbt = at("vbt", [P, 4, T], where=r_at + 22 * K2)
        wct = at("wct", [P, GROUPS, T], where=r_at + 26 * K2)
        mih = at("mih", [P, KT, T], F32R, where=r_at + 28 * K2)
        mil = at("mil", [P, KT, T], F32R, where=r_at + 36 * K2)
        w1c = at("w1c", [P, 2, 16, P], where=r_at + 28 * K2)
        kds = at("kds", [P, 2, GROUPS, T], where=r_at + 36 * K2)
        vswT = at("vswT", [P, 2, T], where=r_at + 40 * K2)
        gateT = at("gateT", [P, T], where=r_at + 42 * K2)
        zc = at("zc", [P, NT, NSA_H, CPAD], where=s_at)
        w2c = at("w2c", [P, 3, HD], where=s_at + 2 * K2)
        hc = at("hc", [P, 2, GROUPS, CPAD], where=s_at + 3 * K2)
        hcr = at("hcr", [P, GROUPS, REP, CPAD], where=s_at + 3 * K2 + 512)
        hx = at("hx", [P, 2, GROUPS * NCMP], where=s_at + 4 * K2)
        z2 = at("z2", [P, 2, ZW], where=s_at)
        wt2 = at("wt2", [P, NT, T], where=s_at + 5 * K2)
        kc = at("kc", [P, GROUPS, CPAD], where=a_at)
        vc = at("vc", [P, GROUPS, HD], where=a_at + 256)
        gt = at("gt", [P, NT, 24], where=a_at + 768)
        bc = at("bc", [P, NT, NSA_H, CPAD], where=n_at)
        dc = at("dc", [P, NT, CPAD], where=n_at + 2 * K2)
        dm2 = at("dm2", [P, T], where=n_at + 3 * K2)
        rb = at("rb", [P, 2, T], where=n_at + 4 * K2)
        nst = at("nst", [P, P], where=n_at + 6 * K2)
        yh = at("yh", [P, KT, T], F32R, where=r_at)
        yl = at("yl", [P, KT, T], F32R, where=r_at + 8 * K2)
        ms = at("ms", [P, 2, T], where=r_at + 16 * K2)
        yf = at("yf", [P, 2, T], where=r_at + 18 * K2)
        onorm = at("onorm", [P, 2, T], where=r_at)
        outb = at("outb", [P, NT, D], where=r_at + 2 * K2)

        sm = at("sm", [P, 160], where=s_at + 9 * K2)
        mxs, nmx, sums, rcs = sm[:, 0:8], sm[:, 8:16], sm[:, 16:24], sm[:, 24:32]
        ssh = sm[:, 32:64]
        rsh = sm[:, 64:96]
        cmx, csm = sm[:, 96:128], sm[:, 128:160]
        okh = cmx
        hb = tiny[:, 48:50]
        lbs, oml = tiny[:, 0:4], tiny[:, 4:8]
        nlam = tiny[:, 8:9]
        lsc = tiny[:, 10:34]
        rv = tiny[:, 40:44]
        epst = tiny[:, 44:45]

        B = [ctx.enter_context(nc.psum_tensor(f"bank{i}", [P, T], F32)) for i in range(8)]

        def sem(name):
            return ctx.enter_context(nc.semaphore(name))

        x_in, vec_in, ada0_in = sem("x_in"), sem("vec_in"), [sem(f"ada0_in{i}") for i in range(8)]
        ct_in = sem("ct_in")
        const_ok, zeroed, vecT, vecT_out = sem("const_ok"), sem("zeroed"), sem("vecT"), sem("vecT_out")
        setup_v, setup_a = sem("setup_v"), sem("setup_a")
        w_in = [sem("w_in0"), sem("w_in1")]
        w_hi, w_split = sem("w_hi"), sem("w_split")
        unit_done = sem("unit_done")
        drain_a, drain_v = sem("drain_a"), sem("drain_v")
        ada_in, mod_step, mod_acc = sem("ada_in"), sem("mod_step"), sem("mod_acc")
        mod_sum, mod_out = sem("mod_sum"), sem("mod_out")
        x_turned = sem("x_turned")
        sq_ok, ssq_ok = sem("sq_ok"), sem("ssq_ok")
        n_sum, n_std, n_rstd = sem("n_sum"), sem("n_std"), sem("n_rstd")
        gain_ok = sem("gain_ok")
        n_t, n_u32, n_uh, n_ul = sem("n_t"), sem("n_u32"), sem("n_uh"), sem("n_ul")
        n_res = sem("n_res")
        silu_ok, h_ok, hh_ok, hl_ok = sem("silu_ok"), sem("h_ok"), sem("hh_ok"), sem("hl_ok")
        g_f, g_k, g_ln, g_bb = sem("g_f"), sem("g_k"), sem("g_ln"), sem("g_bb")
        g_x, g_e, g_qk, g_p, g_a = sem("g_x"), sem("g_e"), sem("g_qk"), sem("g_p"), sem("g_a")
        g_q0, g_kh, g_turn, g_turned = sem("g_q0"), sem("g_kh"), sem("g_turn"), sem("g_turned")
        g_u, g_s, g_o = sem("g_u"), sem("g_s"), sem("g_o")
        g_zero = sem("g_zero")
        ss_ok, rs_ok, o_kept, o_clamped = sem("ss_ok"), sem("rs_ok"), sem("o_kept"), sem("o_clamped")
        mx_n, mx_t, mx_f, mx_h, mx_l = sem("mx_n"), sem("mx_t"), sem("mx_f"), sem("mx_h"), sem("mx_l")
        d_tab, z_ok, zb_ok, m_ok, e_ok = sem("d_tab"), sem("z_ok"), sem("zb_ok"), sem("m_ok"), sem("e_ok")
        r_ok, w_ok, t_ok, wt_ok, pv_ok = sem("r_ok"), sem("w_ok"), sem("t_ok"), sem("wt_ok"), sem("pv_ok")
        v_turn, v_turned = sem("v_turn"), sem("v_turned")
        sb_m, sb_s, sb_r = sem("sb_m"), sem("sb_s"), sem("sb_r")
        pair_ok, mh_ok, ml_ok = sem("pair_ok"), sem("mh_ok"), sem("ml_ok")
        c_in, tab2, c_h, c_hb, c_hx, c_hg = (sem("c_in"), sem("tab2"), sem("c_h"), sem("c_hb"), sem("c_hx"), sem("c_hg"))
        c_kv, c_kvc = sem("c_kv"), sem("c_kvc")
        c_z, c_v, c_e, c_t, c_wt = sem("c_z"), sem("c_v"), sem("c_e"), sem("c_t"), sem("c_wt")
        v2_turn, v2_turned = sem("v2_turn"), sem("v2_turned")
        y_f, y_h, y_l = sem("y_f"), sem("y_h"), sem("y_l")
        o_n, o_t, o_c, stored = sem("o_n"), sem("o_t"), sem("o_c"), sem("stored")

        block = ctx.enter_context(nc.Block())

        def wview(name):
            return t_in[name][0].rearrange("(k p) f -> p k f", p=P)

        W = {n: wview(n) for n in ("w_in", "w_out", "w_ffn_gate", "w_ffn_up", "w_ffn_down", "w_in_2",
                                   "w_proj_a_2", "w_proj_b_2", "w_out_2", "w_ffn_gate_2", "w_ffn_up_2",
                                   "w_ffn_down_2")}
        ADA = [t_in[n][0].rearrange("(p k) f -> p k f", k=KT) for n in ("w_ada", "w_ada_2")]
        DOWN = [(0, 8), (8, 16), (16, 22)]

        def unit_source(name, i, c, snap):
            def ds(first, n):
                return bass.ds(first if isinstance(first, int) else snap(first), n)

            col0 = {"q1": 0, "f1": 512, "i1": 1024, "g1": 1536, "a1": 2048}
            if name in col0:
                return W["w_in"][:, :, ds(i * 256 + (col0[name] + c * P), P)], KT, P
            if name in ("out1", "out2"):
                w = W["w_out" if name == "out1" else "w_out_2"]
                return w[:, :, ds(i * 256 + c * P, P)], KT, P
            if name in ("ff1", "ff2"):
                w = W[("w_ffn_gate", "w_ffn_up")[c] + ("" if name == "ff1" else "_2")]
                return w[:, :, ds(i * P, P)], KT, P
            if name in ("down1", "down2"):
                a, b = DOWN[c % 3]
                w = W["w_ffn_down" if name == "down1" else "w_ffn_down_2"]
                return w[:, a:b, ds(i * 256 + (c // 3) * P, P)], b - a, P
            if name == "qa2":
                return W["w_in_2"][:, :, ds(i * 256 + c * P, P)], KT, P
            if name == "kv2":
                n = P if c < 6 else 24
                return W["w_in_2"][:, :, 512 + c * P:512 + c * P + n], KT, n
            if name == "b2":
                return W["w_in_2"][:, :, ds(i * 256 + (1304 + c * P), P)], KT, P
            if c < 2:
                return W["w_in_2"][:, :, ds(i * P + (2840 + c * D), P)], KT, P
            return W[("w_proj_a_2", "w_proj_b_2")[c - 2]][:, :, ds(i * P, P)], 4, P

        RIDE = {"q1": (0, 8), "f1": (0, 10), "i1": (0, 12), "g1": (0, 14), "a1": (0, 16), "ff1": (1, 0)}
        MOD0 = {"q1": 8, "f1": 10, "i1": 12, "g1": 14, "a1": 16, "tail1": 22, "ff1": 24, "tail2": 46}

        @block.sync
        def _(sp):
            def load_unit(ph, i, c):
                u = i * ph.units + (ph.u0 + c)
                slot = (ph.u0 + c) % 2 if ph.units % 2 == 0 else (ph.u0 + c) % 2
                src, nk, n = unit_source(ph.name, i, c, sp.snap)
                dst = wraw[:, slot, 0:nk * P].rearrange("p (k f) -> p k f", k=nk)[:, :, 0:n]
                if ph.name == "merge2" and c == 1:
                    sp.wait_ge(w_split, u)
                elif not (isinstance(u, int) and u < 2) and not (ph.name == "merge2" and c == 2):
                    sp.wait_ge(w_split, u - 1)
                sp.dma_start(dst, src).then_inc(w_in[slot], 16)

            def load_ada(m, chunk, step):
                first = chunk * MODC if isinstance(chunk, int) else sp.snap(chunk * MODC)
                sp.wait_ge(mod_acc, step)
                sp.dma_start(ada[:], ADA[m][:, :, ds(first, MODC)]).then_inc(ada_in, 16)

            sp.dma_start(xin[:], t_in["x"][0].rearrange("(j p) d -> p j d", p=P)).then_inc(x_in, 16)
            sp.dma_start(ct[:, 0, :], t_in["c"][0].rearrange("(p k) -> p k", k=KT)).then_inc(ct_in, 16)
            sp.dma_start(ct[:, 1, :], t_in["c_2"][0].rearrange("(p k) -> p k", k=KT)).then_inc(ct_in, 16)
            for c in range(8):
                sp.dma_start(ada0[:, c], ADA[0][:, :, c * MODC:(c + 1) * MODC]).then_inc(ada0_in[c], 16)

            def gemm(name, tail=None):
                ph = PH[name]
                if ph.iters == 1:
                    for c in range(ph.units):
                        load_unit(ph, 0, c)
                    return
                start = 0
                if ph.u0 == 0 or tail:
                    body(ph, 0, tail)
                    start = 1
                if start < ph.iters:
                    with sp.Fori(start, ph.iters) as i:
                        body(ph, i)

            def body(ph, i, tail=None):
                for c in range(ph.units):
                    load_unit(ph, i, c)
                    if c == 1 and tail:
                        tail()
                if ph.name in RIDE:
                    m, c0 = RIDE[ph.name]
                    load_ada(m, i + c0, i + MOD0[ph.name])

            for name in ("q1", "f1", "i1", "g1", "a1"):
                gemm(name)
            def mod_tail(m, step):
                return lambda: [load_ada(m, 22 + n, step + n) for n in range(2)]

            def compress_weights():
                sp.wait_ge(n_res, KT)
                for n, (w1, w2) in enumerate((("cmp_w1_k_2", "cmp_w2_k_2"), ("cmp_w1_v_2", "cmp_w2_v_2"))):
                    sp.dma_start(w1c[:, n], t_in[w1][0].rearrange("(j p) h -> p j h", p=P)).then_inc(c_in, 16)
                    sp.dma_start(w2c[:, 2 * n, :], t_in[w2][0]).then_inc(c_in, 16)

            gemm("out1", tail=mod_tail(0, 22))
            gemm("ff1")
            gemm("down1", tail=mod_tail(1, 46))
            gemm("qa2", tail=compress_weights)
            gemm("kv2")
            gemm("b2")
            gemm("merge2")
            gemm("out2")
            gemm("ff2")
            gemm("down2")
            sp.wait_ge(o_c, KT)
            sp.dma_start(out[0].rearrange("(j p) d -> p j d", p=P), outb[:]).then_inc(stored, 16)
            sp.wait_ge(stored, 16)

        @block.gpsimd
        def _(g):
            n = [0]

            def step(ins, signal=const_ok):
                ins.then_inc(signal, 1)
                n[0] += 1
                g.wait_ge(signal, n[0])

            nc.gpsimd.memset(v1[:], 0.0).then_inc(zeroed, 1)
            nc.gpsimd.memset(v2[:], 0.0).then_inc(zeroed, 1)
            g.wait_ge(zeroed, 2)
            row = lambda name, k: t_in[name].rearrange("o (k p) -> (o k) p", p=P)
            loads = [(v1, B_ADA, "b_ada", 48), (v1, NORM_A, "norm1_w", 8), (v1, NORM_B, "norm2_w", 8),
                     (v1, LB, "hgrn_lb_logits", 8), (v1, GNORM, "hgrn_gnorm_w", 1), (v1, SUBLN, "diff_subln_w", 1),
                     (v2, B_ADA, "b_ada_2", 48), (v2, NORM_A, "norm_mix_g_2", 8), (v2, NORM_B, "norm_ffn_g_2", 8)]
            for v, r, name, k in loads:
                g.dma_start(v[r:r + k, :], row(name, k)).then_inc(vec_in, 16)
            for v, name in ((v1, "final_norm_w"), (v2, "norm_final_g_2")):
                g.dma_start(v[NORM_F:NORM_F + 8, :], t_in[name].rearrange("(k p) -> k p", p=P)).then_inc(vec_in, 16)
            for r, name in ((POS_K, "cmp_pos_k_2"), (POS_V, "cmp_pos_v_2")):
                g.dma_start(v2[r:r + 16, :], t_in[name][0].rearrange("(j a) d -> j (a d)", a=2)).then_inc(vec_in, 16)
            for k, name in enumerate(("diff_lambda_q1", "diff_lambda_k1", "diff_lambda_q2", "diff_lambda_k2")):
                g.dma_start(lamv[:, k, :], t_in[name].broadcast_to([P, HD])).then_inc(vec_in, 16)
            step(nc.gpsimd.memset(ident[:], 0.0))
            step(nc.gpsimd.affine_select(out=ident[:], in_=ident[:], compare_op=ALU.not_equal, fill=1.0, base=0,
                                         pattern=[[-1, P]], channel_multiplier=1))
            step(nc.gpsimd.memset(ones[:], 1.0))
            step(nc.gpsimd.memset(epst, EPS))

            def sum_squares(k):
                if k:
                    g.wait_ge(n_sum, k)
                nc.gpsimd.memset(ssq[:], 0.0).then_inc(ssq_ok, 1)
                for t in range(KT):
                    g.wait_ge(sq_ok, KT * k + t + 1)
                    g.wait_ge(ssq_ok, 9 * k + t + 1)
                    nc.gpsimd.tensor_tensor(ssq[:], ssq[:], sq[:, t % 2], ALU.add).then_inc(ssq_ok, 1)

            sum_squares(0)
            g.wait_ge(unit_done, PH["out1"].u0 + U1)
            step(nc.gpsimd.iota(lmask[:, 7, :], [[1, P]], base=0, channel_multiplier=0))
            step(nc.gpsimd.iota(lmask[:, 6, :], [[0, P]], base=0, channel_multiplier=1))
            step(nc.gpsimd.memset(rmask[:], 1.0))
            step(nc.gpsimd.memset(rmask[:, 0:T:P], 0.0))
            step(nc.gpsimd.iota(dm1[:], [[8, T]], base=-8 * 384, channel_multiplier=-8,
                                allow_small_or_imprecise_dtypes=True))
            step(nc.gpsimd.affine_select(out=dm1[:], in_=dm1[:], compare_op=ALU.is_ge, fill=BIG, base=384,
                                         pattern=[[-1, T]], channel_multiplier=1))
            g.wait_ge(mx_l, KT)
            sum_squares(1)
            sum_squares(2)
            sum_squares(3)
            g.wait_ge(n_ul, KT * 3)
            m = [0]

            def step2(ins):
                ins.then_inc(tab2, 1)
                m[0] += 1
                g.wait_ge(tab2, m[0])

            step2(nc.gpsimd.iota(dc[:], [[-8 * P, NT], [8 * CSTRIDE, CPAD]], base=8 * (CBLOCK - 1),
                                 channel_multiplier=-8, allow_small_or_imprecise_dtypes=True))
            step2(nc.gpsimd.affine_select(out=dc[:], in_=dc[:], compare_op=ALU.is_ge, fill=BIG, base=-(CBLOCK - 1),
                                          pattern=[[P, NT], [-CSTRIDE, CPAD]], channel_multiplier=1))
            for h in range(NSA_H):
                step2(nc.gpsimd.tensor_scalar(bc[:, :, h, :], dc[:], 2.0 ** -(h + 1), None, ALU.mult))
            step2(nc.gpsimd.memset(rv, 1.0))
            step2(nc.gpsimd.affine_select(out=rv[:, 0:1], in_=rv[:, 0:1], compare_op=ALU.is_ge, fill=0.0,
                                          base=-(CBLOCK - 1), pattern=[[0, 1]], channel_multiplier=1))
            step2(nc.gpsimd.iota(dm2[:], [[8, T]], base=-8 * 384, channel_multiplier=-8,
                                 allow_small_or_imprecise_dtypes=True))
            step2(nc.gpsimd.affine_select(out=dm2[:], in_=dm2[:], compare_op=ALU.is_ge, fill=BIG, base=384,
                                          pattern=[[-1, T]], channel_multiplier=1))
            step2(nc.gpsimd.memset(nst[:], 0.0))
            step2(nc.gpsimd.affine_select(out=nst[:], in_=nst[:], compare_op=ALU.is_ge, fill=BIG, base=-1,
                                          pattern=[[-1, P]], channel_multiplier=1))
            g.wait_ge(ml_ok, 8)
            sum_squares(4)
            sum_squares(5)

        N_TAB2 = 2 + NSA_H + 2 + 2 + 2

        @block.tensor
        def _(pe):
            def passes(bank, slot, nk, rh, rl, k0, first, last):
                for k in range(nk):
                    a = wh[:, slot, k * P:(k + 1) * P]
                    b = wl[:, slot, k * P:(k + 1) * P]
                    nc.tensor.matmul(bank[:], a, rh[:, k0 + k, :], start=(first and k == 0), stop=False)
                    nc.tensor.matmul(bank[:], a, rl[:, k0 + k, :], start=False, stop=False)
                    mm = nc.tensor.matmul(bank[:], b, rh[:, k0 + k, :], start=False, stop=(last and k == nk - 1))
                mm.then_inc(unit_done, 1)

            def take(ph, i, c):
                pe.wait_ge(w_split, i * ph.units + (ph.u0 + c + 1))
                return (ph.u0 + c) % 2

            def mod_matmuls(step):
                pe.wait_ge(mod_acc, step + 1)
                pe.wait_ge(mod_out, step) if not (isinstance(step, int) and step == 0) else None
                for half in range(2):
                    mm = nc.tensor.matmul(B[5][:, half:half + 1], acc[:, half * P:(half + 1) * P], ones[:, 0:1],
                                          start=True, stop=True)
                mm.then_inc(mod_sum, 1)

            def simple(name, rh, rl, n_ready=None):
                ph = PH[name]
                with pe.Fori(0, ph.iters) as i:
                    for c in range(2):
                        slot = take(ph, i, c)
                        pe.wait_ge(drain_a, i * 2 + (ph.a0 + c - 1))
                        if n_ready is not None and c == 0:
                            pe.wait_ge(n_ul, n_ready)
                        passes(B[(ph.u0 + c) % 2], slot, KT, rh, rl, 0, True, True)
                    if name in RIDE:
                        mod_matmuls(i + MOD0[name])

            def out_proj(name, rh, rl, ready):
                ph = PH[name]
                sem_ready, count = ready
                with pe.Fori(0, ph.iters) as i:
                    for c in range(2):
                        slot = take(ph, i, c)
                        if c == 0:
                            pe.wait_ge(sem_ready, count)
                        pe.wait_ge(drain_v, i * 2 + (ph.d0 + c - 1))
                        passes(B[c], slot, KT, rh, rl, 0, True, True)

            def ffn(name, n_ready, h0):
                ph = PH[name]
                with pe.Fori(0, ph.iters) as i:
                    slot = take(ph, i, 0)
                    pe.wait_ge(n_ul, n_ready)
                    pe.wait_ge(drain_a, i + ph.a0)
                    passes(B[0], slot, KT, uh, ul, 0, True, True)
                    slot = take(ph, i, 1)
                    pe.wait_ge(h_ok, i + h0)
                    passes(B[1], slot, KT, uh, ul, 0, True, True)
                    if name in RIDE:
                        mod_matmuls(i + MOD0[name])

            def down(name, count):
                ph = PH[name]
                with pe.Fori(0, ph.iters) as i:
                    for t in range(2):
                        pe.wait_ge(drain_v, i * 2 + (ph.d0 + t - 1))
                        for c, (a, b) in enumerate(DOWN):
                            slot = take(ph, i, 3 * t + c)
                            if t == 0 and c == 0:
                                pe.wait_ge(hl_ok, count)
                            passes(B[t], slot, b - a, hh, hl, a, c == 0, c == 2)

            def norm(k):
                pe.wait_ge(ssq_ok, 9 * (k + 1))
                nc.tensor.matmul(B[4][:], ones[:], ssq[:], start=True, stop=True).then_inc(n_sum, 1)

            pe.wait_ge(const_ok, 4)
            pe.wait_ge(vec_in, 16 * 17)
            nc.tensor.transpose(B[6][:, 0:P], v1[:], ident[:]).then_inc(unit_done, U1)
            nc.tensor.transpose(B[6][:, P:2 * P], v2[:], ident[:]).then_inc(vecT, 1)
            pe.wait_ge(x_in, 16)
            for k in range(KT):
                if k >= 2:
                    pe.wait_ge(drain_a, k - 1)
                for j in range(NT):
                    mm = nc.tensor.transpose(B[k % 2][:, j * P:(j + 1) * P], xin[:, j, k * P:(k + 1) * P], ident[:])
                mm.then_inc(x_turned, 1)
            norm(0)
            for s in range(8):
                mod_matmuls(s)

            for name in ("q1", "f1", "i1", "g1", "a1"):
                simple(name, uh, ul, KT)
            mod_matmuls(22)
            mod_matmuls(23)
            pe.wait_ge(mod_out, 24)
            pe.wait_ge(drain_a, PH["out1"].a0)

            for h in range(HEADS1):
                q, k, v = p1[:, h, :], p1[:, 4 + h, :], p1[:, 8 + h, :]
                if h:
                    pe.wait_ge(g_turned, 2 * h)
                for c in range(NT):
                    mm = nc.tensor.transpose(B[2][:, c * P:(c + 1) * P], v[:, c * P:(c + 1) * P], ident[:])
                mm.then_inc(g_turn, 1)
                for lv in range(8):
                    n = 8 * h + lv
                    if n >= 4:
                        pe.wait_ge(g_a, n - 3)
                    if lv < 7:
                        pe.wait_ge(g_qk, 2 * (7 * h + lv) + 2)
                    else:
                        pe.wait_ge(g_k, h + 1)
                    lhs, rhs = (kl[:, lv % 2], ql[:, lv % 2]) if lv < 7 else (k, q)
                    for c in range(NT):
                        cc = slice(c * P, (c + 1) * P)
                        mm = nc.tensor.matmul(B[4 + n % 4][:, cc], lhs[:, cc], rhs[:, cc], start=True, stop=True)
                    mm.then_inc(g_p, 1)
                pe.wait_ge(g_kh, h + 1)
                if h:
                    pe.wait_ge(g_s, 3 * h)
                for c in range(NT):
                    mm = nc.tensor.transpose(B[3][:, c * P:(c + 1) * P], kl[:, 1, c * P:(c + 1) * P], ident[:])
                mm.then_inc(g_turn, 1)
                pe.wait_ge(g_turned, 2 * h + 2)
                for c in range(3):
                    cc = slice(c * P, (c + 1) * P)
                    mm = nc.tensor.matmul(B[3][:, cc], kht[:, cc], vtm[:, cc], start=True, stop=True)
                mm.then_inc(g_u, 1)
                pe.wait_ge(g_a, 8 * (h + 1))
                pe.wait_ge(g_q0, h + 1)
                if h >= 2:
                    pe.wait_ge(ss_ok, 4 * (h - 1))
                for c in range(NT):
                    cc = slice(c * P, (c + 1) * P)
                    mm = nc.tensor.matmul(B[h % 2][:, cc], am[:, cc], vtm[:, cc], start=True, stop=(c == 0))
                    if c:
                        pe.wait_ge(g_s, 3 * h + c)
                        mm = nc.tensor.matmul(B[h % 2][:, cc], q0[:, cc], st[:, c - 1, :], start=False, stop=True)
                mm.then_inc(g_o, 1)

            def scores(n, i, q, k):
                nc.tensor.matmul(B[4 + i][:, 0:ZLEN[i]], q[:, i * P:(i + 1) * P], k[:, 0:ZLEN[i]],
                                 start=True, stop=True).then_inc(z_ok, 1)

            def turn_weights(job, i, z):
                kk = 4 * job + i
                pe.wait_ge(w_ok, kk + 1)
                if kk >= 2:
                    pe.wait_ge(wt_ok, kk - 1)
                for j in range(i + 1):
                    mm = nc.tensor.transpose(B[2 + kk % 2][:, j * P:(j + 1) * P],
                                             z[:, ZOFF[i] + j * P:ZOFF[i] + (j + 1) * P], ident[:])
                mm.then_inc(t_ok, 1)

            def map_scores(h, m):
                half = slice(64 * m, 64 * m + 64)
                for i in range(NT):
                    if 2 * h + m:
                        pe.wait_ge(zb_ok, 4 * (2 * h + m - 1) + i + 1)
                    scores(2 * h + m, i, p1[half, 16 + h, :], p1[half, 20 + h, :])

            for s in range(HEADS1 + 1):
                if s < HEADS1:
                    h = s
                    if h == 0:
                        pe.wait_ge(g_a, 32)
                        pe.wait_ge(ss_ok, 16)
                    map_scores(h, 0)
                if s:
                    for i in range(NT):
                        turn_weights(s - 1, i, z1[:, 0])
                if s < HEADS1:
                    map_scores(s, 1)
                if s:
                    h = s - 1
                    if h >= 2:
                        pe.wait_ge(ss_ok, 16 + 4 * (h - 1))
                    for j in range(NT):
                        mm = nc.tensor.transpose(B[h % 2][:, j * P:(j + 1) * P],
                                                 p1[:, 24 + h, j * P:(j + 1) * P], ident[:])
                    mm.then_inc(v_turn, 1)
                    pe.wait_ge(v_turned, h + 1)
                    for i in range(NT):
                        pe.wait_ge(wt_ok, 4 * h + i + 1)
                        for j in range(i + 1):
                            mm = nc.tensor.matmul(B[h % 2][:, i * P:(i + 1) * P],
                                                  wt1[:, h % 2, j, i * P:(i + 1) * P],
                                                  vd1[:, h % 2, j * P:(j + 1) * P], start=(j == 0), stop=(j == i))
                    mm.then_inc(pv_ok, 1)

            for h in range(2 * HEADS1):
                src = p1[:, 8 + h, :] if h < HEADS1 else p1[:, 20 + h, :]
                pe.wait_ge(mx_n, h + 1)
                if h >= 2:
                    pe.wait_ge(mx_f, h - 1)
                else:
                    pe.wait_ge(wt_ok, 16)
                for j in range(NT):
                    mm = nc.tensor.transpose(B[2 + h % 2][:, j * P:(j + 1) * P], src[:, j * P:(j + 1) * P], ident[:])
                mm.then_inc(mx_t, 1)

            out_proj("out1", mixh, mixl, (mx_l, KT))
            norm(1)
            ffn("ff1", 2 * KT, H1)
            mod_matmuls(46)
            mod_matmuls(47)
            down("down1", FT)
            norm(2)
            norm(3)

            simple("qa2", uh, ul, 3 * KT)
            ph = PH["kv2"]
            for c in range(7):
                slot = take(ph, 0, c)
                pe.wait_ge(drain_a, ph.a0 + c - 1)
                passes(B[(ph.u0 + c) % 2], slot, KT, uh, ul, 0, True, True)
            simple("b2", uh, ul)
            nturn = 0
            for n in range(7):
                if n >= 2:
                    pe.wait_ge(v2_turned, n - 1)
                elif n == 0:
                    pe.wait_ge(drain_a, PH["merge2"].a0)
                for j in range(NT):
                    src = (vswT[:, n] if n < 2 else gateT[:] if n == 2 else qkvb[:, 8 + n - 3])
                    mm = nc.tensor.transpose(B[2 + n % 2][:, j * P:(j + 1) * P], src[:, j * P:(j + 1) * P], ident[:])
                mm.then_inc(v2_turn, 1)
            pe.wait_ge(c_in, 64)
            for n in range(2):
                for jj in range(16):
                    nc.tensor.matmul(B[4 + n][:, 0:GROUPS * NCMP].rearrange("p (g n) -> p g n", g=GROUPS),
                                     w1c[:, n, jj, :],
                                     kds[:, n, :, 2 * jj:2 * jj + CSTRIDE * (NCMP - 1) + 1:CSTRIDE],
                                     start=(jj == 0), stop=(jj == 15))
                pos = (POS_K, POS_V)[n]
                for jj in range(16):
                    mm = nc.tensor.matmul(B[6 + n][:, 0:1], w1c[:, n, jj, :], vt2[:, pos + jj:pos + jj + 1],
                                          start=(jj == 0), stop=(jj == 15))
                mm.then_inc(c_h, 1)
            pe.wait_ge(c_hg, 2)
            pe.wait_ge(v2_turned, 7)
            nc.tensor.matmul(B[2][:, 0:GROUPS * CPAD], w2c[:, 0:2, :].rearrange("p a d -> p (a d)"),
                             hc[:, 0].rearrange("p g n -> p (g n)"), start=True, stop=True)
            pe.wait_ge(c_hg, 3)
            for g_ in range(GROUPS):
                mm = nc.tensor.matmul(B[3][:, g_ * HD:(g_ + 1) * HD], hcr[:, g_].rearrange("p r n -> p (r n)"),
                                      w2c[:, 2, :], start=True, stop=True)
            mm.then_inc(c_kv, 1)
            pe.wait_ge(c_kvc, 2)
            for i in range(NT):
                for h in range(NSA_H):
                    half = slice(64 * (h % 2), 64 * (h % 2) + 64)
                    col = (i * REP + h // 2) * CPAD
                    mm = nc.tensor.matmul(B[6 + h % 2][:, col:col + CPAD], qa[half, h // 2, i * P:(i + 1) * P],
                                          kc[half, h // REP, :], start=True, stop=True)
            mm.then_inc(c_z, 1)
            pe.wait_ge(c_e, 6)
            for g_ in range(GROUPS):
                for i in range(NT):
                    mm = nc.tensor.transpose(B[2 + g_][:, i * P:(i + 1) * P],
                                             zc[:, i, g_ * REP:(g_ + 1) * REP, :].rearrange("p r n -> p (r n)"),
                                             ident[:])
            mm.then_inc(c_t, 1)
            pe.wait_ge(c_wt, 1)

            def unit_operands(n):
                if n < 24:
                    h, br = (n - 8) // 2, (n - 8) % 2
                    half = slice(64 * (h % 2), 64 * (h % 2) + 64)
                    return qa[half, h // 2, :], kdup[half, br, h // REP, :]
                h = n - 24
                half = slice(64 * (h % 2), 64 * (h % 2) + 64)
                return qkvb[half, h // 2, :], qkvb[half, 4 + h // 2, :]

            for s in range(8, 33):
                if s < 32:
                    q, k = unit_operands(s)
                    for i in range(NT):
                        if s > 24:
                            pe.wait_ge(sb_s, 2 * (4 * (s - 25) + i + 1))
                        else:
                            pe.wait_ge(zb_ok, 4 * (s - 1) + i + 1)
                        scores(s, i, q, k)
                if s > 8:
                    n = s - 1
                    job = n - 4
                    for i in range(NT):
                        turn_weights(job, i, z2[:, n % 2] if n < 24 else z2[:, 1])
                    h = (n - 8) // 2 if n < 24 else n - 24
                    pair = h // 2 if n < 24 else 4 + h // 2
                    rows = slice(64 * (h % 2), 64 * (h % 2) + 64)
                    o = B[pair % 2]
                    if h % 2 == 0 and (n >= 24 or (n - 8) % 2 == 0) and pair >= 2:
                        pe.wait_ge(ml_ok, pair - 1)
                    if n < 24 and (n - 8) % 2 == 0:
                        r = h % REP
                        nc.tensor.matmul(o[rows, :], vc[CPAD * r:CPAD * (r + 1), h // REP, :],
                                         wct[CPAD * r:CPAD * (r + 1), h // REP, :], start=True, stop=False)
                    pe.wait_ge(wt_ok, 4 * (job + 1))
                    for j in range(NT):
                        if n < 24:
                            v = vsw[:, (n - 8) % 2, j * P + HD * (h // REP):j * P + HD * (h // REP) + HD]
                        else:
                            v = vbt[:, h // 2, j * P + HD * (h % 2):j * P + HD * (h % 2) + HD]
                        last = j == NT - 1 and (n >= 24 or (n - 8) % 2 == 1)
                        mm = nc.tensor.matmul(o[rows, j * P:T], v, wt2[:, j, j * P:T],
                                              start=(n >= 24 and j == 0), stop=last)
                    mm.then_inc(pv_ok, 1)

            pe.wait_ge(ml_ok, 8)
            ph = PH["merge2"]
            with pe.Fori(0, ph.iters) as i:
                for c in range(4):
                    slot = take(ph, i, c)
                    if c < 2:
                        pe.wait_ge(drain_a, i * 2 + (ph.a0 + c))
                        passes(B[c], slot, KT, uh, ul, 0, True, True)
                    else:
                        pe.wait_ge(drain_v, i * 2 + (ph.d0 + c - 2))
                        passes(B[c], slot, 4, mih, mil, 4 * (c - 2), True, True)
            out_proj("out2", yh, yl, (y_l, KT))
            norm(4)
            ffn("ff2", 4 * KT, H1 + FT)
            down("down2", 2 * FT)
            norm(5)
            for k in range(KT):
                pe.wait_ge(o_n, k + 1)
                if k >= 2:
                    pe.wait_ge(o_c, k - 1)
                for j in range(NT):
                    mm = nc.tensor.transpose(B[k % 2][:, j * P:(j + 1) * P], onorm[:, k % 2, j * P:(j + 1) * P],
                                             ident[:])
                mm.then_inc(o_t, 1)

        @block.scalar
        def _(act):
            A = nc.scalar.activation

            def square_res(k, t, tile):
                if not (isinstance(t, int) and k == 0 and t < 2):
                    act.wait_ge(ssq_ok, t + (9 * k))

            def norm_std(k):
                act.wait_ge(n_sum, k + 1)
                A(sq[:, 0], B[4][:], ACT.Sqrt, bias=epst, scale=1.0 / D).then_inc(n_std, 1)

            def norm_u(k, nu, shift):
                act.wait_ge(gain_ok, nu + 1)
                for t in range(KT):
                    c = t % 2
                    act.wait_ge(n_t, KT * nu + t + 1)
                    if KT * nu + t >= 2:
                        act.wait_ge(n_ul, KT * nu + t - 1)
                    A(u32[:, c], tn[:, c], ACT.Identity, bias=shift[:, t:t + 1],
                      scale=gain[:, nu, t:t + 1]).then_inc(n_u32, 1)
                    A(uh[:, t, :], tn[:, c], ACT.Identity, bias=shift[:, t:t + 1],
                      scale=gain[:, nu, t:t + 1]).then_inc(n_uh, 1)

            def mod_drain(m, chunk, step):
                modt, vt = (mod1, vt1) if m == 0 else (mod2, vt2)
                act.wait_ge(mod_sum, step + 1)
                A(modt[:, ds(chunk * 2, 1)], B[5][:, 0:1], ACT.Identity, bias=vt[:, ds(chunk * 2, 1)])
                A(modt[:, ds(chunk * 2 + 1, 1)], B[5][:, 1:2], ACT.Identity,
                  bias=vt[:, ds(chunk * 2 + 1, 1)]).then_inc(mod_out, 1)

            def drain(name, dst, col0, func):
                ph = PH[name]
                with act.Fori(0, ph.iters) as i:
                    for c in range(2):
                        act.wait_ge(unit_done, i * 2 + (ph.u0 + c + 1) + U1)
                        A(dst[:, ds(i * 2 + (col0 + c), 1), :].rearrange("p a t -> p (a t)"),
                          B[(ph.u0 + c) % 2][:], func).then_inc(drain_a, 1)
                    if name in RIDE:
                        m, c0 = RIDE[name]
                        mod_drain(m, i + c0, i + MOD0[name])

            def residual_squares(name, k):
                ph = PH[name]
                with act.Fori(0, ph.iters) as i:
                    for c in range(2):
                        act.wait_ge(drain_v, i * 2 + (ph.d0 + c + 1))
                        act.wait_ge(ssq_ok, i * 2 + (9 * k + c))
                        A(sq[:, c], res[:, ds(i * 2 + c, 1), :].rearrange("p a t -> p (a t)"),
                          ACT.Square).then_inc(sq_ok, 1)

            def ffn(name, base):
                ph = PH[name]
                with act.Fori(0, ph.iters) as i:
                    act.wait_ge(unit_done, i * 2 + (ph.u0 + 1) + U1)
                    A(sg[:, 0], B[0][:], ACT.Silu).then_inc(drain_a, 1)
                    act.wait_ge(h_ok, i + (base + H1 + 1))
                    A(hh[:, ds(i, 1), :].rearrange("p a t -> p (a t)"), hf[:, 0], ACT.Copy).then_inc(hh_ok, 1)
                    if name in RIDE:
                        m, c0 = RIDE[name]
                        mod_drain(m, i + c0, i + MOD0[name])

            act.wait_ge(ct_in, 32)
            A(sc_c[:], ct[:], ACT.Silu).then_inc(setup_a, 1)
            act.wait_ge(vecT, 1)
            A(vt1[:], B[6][:, 0:P], ACT.Copy)
            A(vt2[:], B[6][:, P:2 * P], ACT.Copy).then_inc(vecT_out, 1)
            for k in range(KT):
                act.wait_ge(x_turned, k + 1)
                A(res[:, k, :], B[k % 2][:], ACT.Copy).then_inc(drain_a, 1)
                act.wait_ge(drain_a, k + 1)
                if k >= 2:
                    act.wait_ge(ssq_ok, k)
                A(sq[:, k % 2], res[:, k, :], ACT.Square).then_inc(sq_ok, 1)
            act.wait_ge(setup_v, 5)
            A(lsc[:, 4:12], lsc[:, 4:12], ACT.Exp)
            A(lsc[:, 20:22], lsc[:, 20:22], ACT.Exp).then_inc(setup_a, 1)
            norm_std(0)
            act.wait_ge(vecT_out, 1)
            for s in range(8):
                mod_drain(0, s, s)
            norm_u(0, 0, mod1[:, 0:8])
            drain("q1", p1, 0, ACT.Copy)
            drain("f1", p1, 4, ACT.Sigmoid)
            drain("i1", p1, 8, ACT.Copy)
            drain("g1", p1, 12, ACT.Silu)
            drain("a1", p1, 16, ACT.Copy)
            mod_drain(0, 22, 22)
            mod_drain(0, 23, 23)

            for h in range(HEADS1):
                act.wait_ge(g_turn, 2 * h + 1)
                if h:
                    act.wait_ge(g_o, h)
                A(vtm[:], B[2][:], ACT.Copy).then_inc(g_turned, 1)
                act.wait_ge(g_k, h + 1)
                A(ff[:], ff[:], ACT.Ln).then_inc(g_ln, 1)
                for lv in range(9):
                    act.wait_ge(g_x, 9 * h + lv + 1)
                    if lv == 8:
                        A(xx[:, 0], xx[:, 0], ACT.Exp).then_inc(g_e, 1)
                    elif lv == 7:
                        A(xx[:, 1], bb[:], ACT.Exp).then_inc(g_e, 1)
                    else:
                        A(xx[:, lv % 2], xx[:, lv % 2], ACT.Exp).then_inc(g_e, 1)
                act.wait_ge(g_turn, 2 * h + 2)
                A(kht[:], B[3][:], ACT.Copy).then_inc(g_turned, 1)
                act.wait_ge(g_o, h + 1)
                A(p1[:, 8 + h, :], B[h % 2][:], ACT.Copy)
                for c in range(NT):
                    if h or c:
                        act.wait_ge(ss_ok, 4 * h + c)
                    mm = A(junk[:, 0:P], B[h % 2][:, c * P:(c + 1) * P], ACT.Square,
                           scale=SQ_SCALE, accum_out=ssh[:, 4 * h + c:4 * h + c + 1])
                    mm.then_inc(ss_ok, 1)

            def exps(n, i, z):
                act.wait_ge(m_ok, 4 * n + i + 1)
                c = 4 * (n % 2) + i
                sl = z[:, ZOFF[i]:ZOFF[i] + ZLEN[i]]
                A(sl, sl, ACT.Exp, bias=nmx[:, c:c + 1], scale=SCALE,
                  accum_out=sums[:, c:c + 1]).then_inc(e_ok, 1)

            def take_turned(job, i, wt):
                kk = 4 * job + i
                act.wait_ge(t_ok, kk + 1)
                A(wt[:, 0:i + 1, i * P:(i + 1) * P],
                  B[2 + kk % 2][:, 0:ZLEN[i]].rearrange("p (j t) -> p j t", j=i + 1), ACT.Copy).then_inc(wt_ok, 1)

            for s in range(HEADS1 + 1):
                if s:
                    for i in range(NT):
                        if i == 0 and s >= 3:
                            act.wait_ge(pv_ok, s - 2)
                        take_turned(s - 1, i, wt1[:, (s - 1) % 2])
                if s < HEADS1:
                    for m in range(2):
                        for i in range(NT):
                            exps(2 * s + m, i, z1[:, m])
                if s:
                    h = s - 1
                    act.wait_ge(v_turn, h + 1)
                    A(vd1[:, h % 2], B[h % 2][:], ACT.Copy).then_inc(v_turned, 1)
                    act.wait_ge(pv_ok, h + 1)
                    A(p1[:, 24 + h, :], B[h % 2][:], ACT.Copy).then_inc(o_kept, 1)
                    act.wait_ge(o_clamped, h + 1)
                    for c in range(NT):
                        act.wait_ge(ss_ok, 16 + 4 * h + c)
                        A(junk1[:, 0:P], clamped[:, c * P:(c + 1) * P], ACT.Square, scale=SQ_SCALE,
                          accum_out=ssh[:, 16 + 4 * h + c:17 + 4 * h + c]).then_inc(ss_ok, 1)
            act.wait_ge(rs_ok, 2)
            A(rsh, ssh, ACT.Sqrt, bias=epst, scale=SQ_BACK / P).then_inc(rs_ok, 1)
            for h in range(2 * HEADS1):
                act.wait_ge(mx_f, h + 1)
                A(mixh[:, h, :], z1[:, h % 2, 0:T], ACT.Copy).then_inc(mx_h, 1)

            act.wait_ge(mx_l, KT)
            residual_squares("out1", 1)
            norm_std(1)
            norm_u(1, 1, mod1[:, 24:32])
            ffn("ff1", 0)
            mod_drain(1, 22, 46)
            mod_drain(1, 23, 47)
            residual_squares("down1", 2)
            norm_std(2)
            for t in range(KT):
                act.wait_ge(n_res, t + 1)
                act.wait_ge(ssq_ok, 9 * 3 + t)
                A(sq[:, t % 2], res[:, t, :], ACT.Square).then_inc(sq_ok, 1)
            norm_std(3)
            norm_u(3, 2, mod2[:, 0:8])

            drain("qa2", qa, 0, ACT.Copy)
            ph = PH["kv2"]
            for c in range(7):
                bank = B[(ph.u0 + c) % 2]
                act.wait_ge(unit_done, ph.u0 + c + 1 + U1)
                if c < 2:
                    for g_ in range(GROUPS):
                        A(kds[0:64, c, g_, :], bank[64 * g_:64 * g_ + 64, :], ACT.Copy)
                        mm = A(kds[64:128, c, g_, 0:T - 1], bank[64 * g_:64 * g_ + 64, 1:T], ACT.Copy)
                elif c in (2, 4):
                    for g_ in range(GROUPS):
                        for half in range(2):
                            mm = A(kdup[64 * half:64 * half + 64, c // 2 - 1, g_, :],
                                   bank[64 * g_:64 * g_ + 64, :], ACT.Copy)
                elif c in (3, 5):
                    mm = A(vswT[:, c // 2 - 1, :], bank[:], ACT.Copy)
                else:
                    mm = A(gateT[:], bank[:], ACT.Sigmoid)
                mm.then_inc(drain_a, 1)
            drain("b2", qkvb, 0, ACT.Copy)
            act.wait_ge(tab2, N_TAB2)
            for n in range(7):
                act.wait_ge(v2_turn, n + 1)
                bank = B[2 + n % 2]
                if n == 2:
                    mm = A(gt[:], bank[:].rearrange("p (i c) -> p i c", i=NT)[:, :, 0:24], ACT.Copy)
                else:
                    mm = A(vsw[:, n] if n < 2 else vbt[:, n - 3], bank[:], ACT.Copy)
                mm.then_inc(v2_turned, 1)
            for n in range(2):
                act.wait_ge(c_hx, n + 1)
                A(hc[:, n, :, 0:NCMP], hx[:, n].rearrange("p (g n) -> p g n", g=GROUPS),
                  ACT.Gelu_apprx_tanh).then_inc(c_hg, 1)
            act.wait_ge(c_hg, 2)
            for r in range(REP):
                mm = A(hcr[:, :, r, :], hc[:, 1], ACT.Copy)
            mm.then_inc(c_hg, 1)
            act.wait_ge(c_kv, 1)
            A(kc[:], B[2][:, 0:GROUPS * CPAD].rearrange("p (g n) -> p g n", g=GROUPS), ACT.Copy).then_inc(c_kvc, 1)
            A(vc[:], B[3][:, 0:P].rearrange("p (g d) -> p g d", g=GROUPS), ACT.Copy).then_inc(c_kvc, 1)
            act.wait_ge(c_v, 4)
            zcf = zc[:].rearrange("p i h n -> p (i h n)")
            A(zcf, zcf, ACT.Exp, scale=SCALE).then_inc(c_e, 1)
            act.wait_ge(c_t, 1)
            A(wct[:, 0], B[2][:], ACT.Copy)
            A(wct[:, 1], B[3][:], ACT.Copy).then_inc(c_wt, 1)

            def take_unit(n):
                job = n - 4
                act.wait_ge(pv_ok, job)
                for i in range(NT):
                    take_turned(job, i, wt2)

            def take_pair(n):
                pair = (n - 8) // 4 if n < 24 else 4 + (n - 24) // 2
                if (n < 24 and (n - 8) % 4 == 3) or (n >= 24 and n % 2 == 1):
                    act.wait_ge(pv_ok, n - 3)
                    A(mih[:, pair, :], B[pair % 2][:], ACT.Copy).then_inc(mh_ok, 1)

            for s in range(8, 33):
                if s < 24:
                    for i in range(NT):
                        exps(s, i, z2[:, s % 2])
                    if s > 8:
                        take_unit(s - 1)
                else:
                    take_unit(s - 1)
                    if s < 32:
                        for i in range(NT):
                            k = 4 * (s - 24) + i
                            act.wait_ge(sb_m, k + 1)
                            sl = slice(ZOFF[i], ZOFF[i] + ZLEN[i])
                            A(z2[:, 0, sl], B[4 + i][:, 0:ZLEN[i]], ACT.Sigmoid, scale=-SCALE).then_inc(sb_s, 1)
                            A(z2[:, 1, sl], B[4 + i][:, 0:ZLEN[i]], ACT.Sigmoid, scale=SCALE).then_inc(sb_s, 1)
                if s > 8:
                    take_pair(s - 1)

            act.wait_ge(ml_ok, 8)
            ph = PH["merge2"]
            with act.Fori(0, ph.iters) as i:
                for c in range(2):
                    act.wait_ge(unit_done, i * 4 + (ph.u0 + c + 1) + U1)
                    act.wait_ge(y_f, i + Y1)
                    A(ms[:, c], B[c][:], ACT.Sigmoid).then_inc(drain_a, 1)
                act.wait_ge(y_f, i + (Y1 + 1))
                A(yh[:, ds(i, 1), :].rearrange("p a t -> p (a t)"), yf[:, 0], ACT.Copy).then_inc(y_h, 1)
            residual_squares("out2", 4)
            norm_std(4)
            norm_u(4, 3, mod2[:, 24:32])
            ffn("ff2", FT)
            residual_squares("down2", 5)
            norm_std(5)
            for k in range(KT):
                act.wait_ge(o_t, k + 1)
                A(outb[:, :, k * P:(k + 1) * P], B[k % 2][:].rearrange("p (j f) -> p j f", j=NT),
                  ACT.Copy).then_inc(o_c, 1)

        @block.vector
        def _(v):
            V = nc.vector
            seq = [0]

            def split(u, slot):
                first = isinstance(u, int) and u < 2
                if isinstance(u, int):
                    v.wait_ge(w_in[slot], 16 * (u // 2 + 1))
                if not first:
                    v.wait_ge(unit_done, u - 1 + U1)
                V.tensor_copy(wh[:, slot], wraw[:, slot]).then_inc(w_hi, 1)
                v.wait_ge(w_hi, u + 1)
                V.tensor_tensor(wl[:, slot], wraw[:, slot], wh[:, slot].bitcast(F32), ALU.subtract).then_inc(w_split, 1)

            def ahead(ph, i, c):
                uc = ph.u0 + c + 1
                slot = uc % 2
                if isinstance(i, int):
                    split(i * ph.units + uc, slot)
                    return
                u = i * ph.units + uc
                v.wait_ge(w_in[slot], i * (8 * ph.units) + 16 * (uc // 2 + 1))
                v.wait_ge(unit_done, u - 1 + U1)
                V.tensor_copy(wh[:, slot], wraw[:, slot]).then_inc(w_hi, 1)
                v.wait_ge(w_hi, u + 1)
                V.tensor_tensor(wl[:, slot], wraw[:, slot], wh[:, slot].bitcast(F32), ALU.subtract).then_inc(w_split, 1)

            def mod_products(m, src, step):
                s0 = seq[0]
                if isinstance(step, int):
                    if step:
                        v.wait_ge(mod_sum, step)
                else:
                    v.wait_ge(mod_sum, step)
                for k in range(KT):
                    if k == 0:
                        ins = V.tensor_scalar(acc[:], src[:, 0, :], sc_c[:, m, 0:1], None, ALU.mult)
                    else:
                        v.wait_ge(mod_step, step * (KT - 1) + k)
                        ins = V.scalar_tensor_tensor(acc[:], src[:, k, :], sc_c[:, m, k:k + 1], acc[:],
                                                     op0=ALU.mult, op1=ALU.add)
                    ins.then_inc(mod_step if k < KT - 1 else mod_acc, 1)

            def ride(name, i):
                if name in RIDE:
                    m, _ = RIDE[name]
                    s = i + MOD0[name]
                    v.wait_ge(ada_in, i * 16 + 16 * (MOD0[name] - 7))
                    mod_products(m, ada, s)

            def loop(ph, body):
                with v.Fori(0, ph.iters) as i:
                    body(i)

            def plain(name):
                ph = PH[name]

                def body(i):
                    for c in range(ph.units):
                        ahead(ph, i, c)
                    ride(name, i)
                loop(ph, body)

            def add_residual(name, gates, skip_last=False):
                ph = PH[name]
                per = ph.units // 2

                def body(i, last=False):
                    for t in range(2):
                        for c in range(per):
                            if not (last and t == 1 and c == per - 1):
                                ahead(ph, i, t * per + c)
                        v.wait_ge(unit_done, i * ph.units + (ph.u0 + (t + 1) * per) + U1)
                        if isinstance(i, int):
                            r, gcol = res[:, 2 * i + t, :], gates[:, 2 * i + t:2 * i + t + 1]
                        else:
                            r = res[:, ds(i * 2 + t, 1), :].rearrange("p a t -> p (a t)")
                            gcol = gates[:, ds(i * 2 + t, 1)]
                        V.scalar_tensor_tensor(r, B[t][:], gcol, r, op0=ALU.mult, op1=ALU.add).then_inc(drain_v, 1)
                if not skip_last:
                    loop(ph, body)
                else:
                    with v.Fori(0, ph.iters - 1) as i:
                        body(i)
                    body(ph.iters - 1, last=True)

            def norm_rstd(k):
                v.wait_ge(n_std, k + 1)
                V.reciprocal(rstd[:], sq[:, 0]).then_inc(n_rstd, 1)
                v.wait_ge(n_rstd, k + 1)

            def norm_u(nu):
                for t in range(KT + 1):
                    if t < KT:
                        if KT * nu + t >= 2:
                            v.wait_ge(n_uh, KT * nu + t - 1)
                        V.tensor_tensor(tn[:, t % 2], res[:, t, :], rstd[:], ALU.mult).then_inc(n_t, 1)
                    if t:
                        s = t - 1
                        v.wait_ge(n_uh, KT * nu + s + 1)
                        V.tensor_tensor(ul[:, s, :], u32[:, s % 2], uh[:, s, :].bitcast(F32),
                                        ALU.subtract).then_inc(n_ul, 1)

            def gains(nu, modt, vt, norm_row, sc_col):
                V.scalar_tensor_tensor(gain[:, nu, :], modt[:, sc_col:sc_col + 8], 1.0,
                                       vt[:, norm_row:norm_row + 8], op0=ALU.add, op1=ALU.mult).then_inc(gain_ok, 1)

            def ffn(name, base):
                ph = PH[name]

                def body(i):
                    ahead(ph, i, 0)
                    ahead(ph, i, 1)
                    v.wait_ge(unit_done, i * 2 + (ph.u0 + 2) + U1)
                    v.wait_ge(drain_a, i + (ph.a0 + 1))
                    V.tensor_tensor(hf[:, 0], sg[:, 0], B[1][:], ALU.mult).then_inc(h_ok, 1)
                    v.wait_ge(hh_ok, i + (base + 1))
                    V.tensor_tensor(hl[:, ds(i, 1), :].rearrange("p a t -> p (a t)"), hf[:, 0],
                                    hh[:, ds(i, 1), :].rearrange("p a t -> p (a t)").bitcast(F32),
                                    ALU.subtract).then_inc(hl_ok, 1)
                    ride(name, i)
                loop(ph, body)

            sv = [0]

            def link(ins):
                ins.then_inc(setup_v, 1)
                sv[0] += 1
                v.wait_ge(setup_v, sv[0])

            V.memset(tiny[:, 45:46], 0.0).then_inc(drain_v, 2)
            V.memset(tiny[:, 46:47], 0.0).then_inc(h_ok, H1)
            V.memset(tiny[:, 47:48], 0.0).then_inc(y_f, Y1)
            v.wait_ge(setup_a, 1)
            v.wait_ge(vecT_out, 1)
            l0, l1 = vt1[:, LB:LB + 4], vt1[:, LB + 4:LB + 8]
            link(V.tensor_tensor(lsc[:, 0:4], l0, l1, ALU.max))
            link(V.tensor_tensor(lsc[:, 4:8], l0, lsc[:, 0:4], ALU.subtract))
            link(V.tensor_tensor(lsc[:, 8:12], l1, lsc[:, 0:4], ALU.subtract))
            for m in range(2):
                link(V.tensor_tensor_reduce(lamv[:, 2 * m, :], lamv[:, 2 * m, :], lamv[:, 2 * m + 1, :], 1.0, 0.0,
                                            ALU.mult, ALU.add, lsc[:, 20 + m:21 + m]))
            v.wait_ge(setup_a, 2)
            link(V.tensor_tensor(lsc[:, 12:16], lsc[:, 4:8], lsc[:, 8:12], ALU.add))
            link(V.reciprocal(lsc[:, 16:20], lsc[:, 12:16]))
            link(V.tensor_tensor(lbs, lsc[:, 4:8], lsc[:, 16:20], ALU.mult))
            link(V.tensor_scalar(oml, lbs, -1.0, 1.0, ALU.mult, ALU.add))
            link(V.tensor_tensor(lsc[:, 22:23], lsc[:, 20:21], lsc[:, 21:22], ALU.subtract))
            link(V.tensor_scalar(nlam, lsc[:, 22:23], LAMBDA_INIT, -1.0, ALU.add, ALU.mult))
            for s in range(8):
                v.wait_ge(ada0_in[s], 16)
                mod_products(0, ada0[:, s], s)
            split(0, 0)
            norm_rstd(0)
            v.wait_ge(mod_out, 8)
            gains(0, mod1, vt1, NORM_A, 8)
            norm_u(0)
            for name in ("q1", "f1", "i1", "g1", "a1"):
                plain(name)
            for s in (22, 23):
                v.wait_ge(ada_in, 16 * (s - 7))
                mod_products(0, ada, s)

            v.wait_ge(const_ok, 4 + 6)
            mk = [0]

            def mlink(ins):
                ins.then_inc(g_zero, 1)
                mk[0] += 1
                v.wait_ge(g_zero, mk[0])

            S_, T_ = lmask[:, 6, :], lmask[:, 7, :]
            scr = junk[:].bitcast(I32)
            gtm, xor, ge, lt = scr[:, 0:P], scr[:, P:2 * P], scr[:, 2 * P:3 * P], scr[:, 3 * P:4 * P]
            mlink(V.tensor_tensor(gtm, T_, S_, ALU.is_gt))
            mlink(V.tensor_tensor(xor, T_, S_, ALU.bitwise_xor))
            mlink(V.tensor_scalar(lmask[:, 7, :], xor, 0.0, None, ALU.is_equal))
            for lv, m in enumerate(LEVELS):
                mlink(V.tensor_scalar(ge, xor, float(m), None, ALU.is_ge))
                mlink(V.tensor_scalar(lt, xor, float(2 * m), None, ALU.is_lt))
                mlink(V.tensor_tensor(ge, ge, lt, ALU.mult))
                mlink(V.tensor_tensor(lmask[:, lv, :], ge, gtm, ALU.mult))
            mlink(V.memset(ql[:], 0.0))
            mlink(V.memset(kl[:], 0.0))
            mlink(V.memset(am[:], 0.0))

            for h in range(HEADS1):
                q, fk = p1[:, h, :], p1[:, 4 + h, :]
                if h == 0:
                    v.wait_ge(drain_a, PH["out1"].a0)
                V.tensor_scalar(ff[:], fk, oml[:, h:h + 1], lbs[:, h:h + 1], ALU.mult, ALU.add).then_inc(g_f, 1)
                v.wait_ge(g_f, h + 1)
                V.tensor_scalar(fk, ff[:], -1.0, 1.0, ALU.mult, ALU.add).then_inc(g_k, 1)
                v.wait_ge(g_ln, h + 1)
                V.tensor_tensor_scan(bb[:], rmask[:], ff[:], 0.0, ALU.mult, ALU.add).then_inc(g_bb, 1)
                v.wait_ge(g_bb, h + 1)

                def exponents(lv):
                    m = LEVELS[lv]
                    bv = bb[:].rearrange("p (n c) -> p n c", c=2 * m)
                    xv = xx[:, lv % 2].rearrange("p (n c) -> p n c", c=2 * m)
                    ref = bv[:, :, m - 1:m].broadcast_to([P, T // (2 * m), m])
                    V.tensor_tensor(xv[:, :, m:2 * m], bv[:, :, m:2 * m], ref, ALU.subtract)
                    V.tensor_tensor(xv[:, :, 0:m], ref, bv[:, :, 0:m], ALU.subtract).then_inc(g_x, 1)

                def products(lv):
                    m = LEVELS[lv]
                    n = 7 * h + lv
                    v.wait_ge(g_e, 9 * h + lv + 1)
                    if n >= 2:
                        v.wait_ge(g_p, 8 * h + lv - 1 if lv >= 2 else 8 * (h - 1) + 8)
                    if h and lv < 2:
                        v.wait_ge(g_turn, 2 * h)
                    ev = xx[:, lv % 2].rearrange("p (n c) -> p n c", c=2 * m)
                    for dst, src, a in ((ql, q, m), (kl, fk, 0)):
                        dv = dst[:, lv % 2].rearrange("p (n c) -> p n c", c=2 * m)
                        sv_ = src.rearrange("p (n c) -> p n c", c=2 * m)
                        V.tensor_tensor(dv[:, :, a:a + m], sv_[:, :, a:a + m], ev[:, :, a:a + m],
                                        ALU.mult).then_inc(g_qk, 1)

                def merge(lv):
                    n = 8 * h + lv
                    v.wait_ge(g_p, n + 1)
                    if n:
                        v.wait_ge(g_a, n)
                    if h and lv == 0:
                        v.wait_ge(g_o, h)
                    V.copy_predicated(am[:].rearrange("p (c t) -> p c t", c=NT),
                                      lmask[:, lv, :].unsqueeze(1).broadcast_to([P, NT, P]),
                                      B[4 + n % 4][:].rearrange("p (c t) -> p c t", c=NT)).then_inc(g_a, 1)

                exponents(0)
                for lv in range(7):
                    if lv + 1 < 7:
                        if lv:
                            v.wait_ge(g_qk, 2 * (7 * h + lv))
                        exponents(lv + 1)
                    products(lv)
                    if lv:
                        merge(lv - 1)
                v.wait_ge(g_qk, 14 * (h + 1))
                V.tensor_tensor(xx[:, 0].rearrange("p (c t) -> p c t", c=NT),
                                bb[:].rearrange("p (c t) -> p c t", c=NT)[:, :, P - 1:P].broadcast_to([P, NT, P]),
                                bb[:].rearrange("p (c t) -> p c t", c=NT), ALU.subtract).then_inc(g_x, 2)
                merge(6)
                v.wait_ge(g_e, 9 * h + 8)
                if h:
                    v.wait_ge(g_o, h)
                V.tensor_tensor(q0[:], q, xx[:, 1], ALU.mult).then_inc(g_q0, 1)
                v.wait_ge(g_e, 9 * h + 9)
                v.wait_ge(g_p, 8 * h + 8)
                V.tensor_tensor(kl[:, 1], fk, xx[:, 0], ALU.mult).then_inc(g_kh, 1)
                merge(7)
                v.wait_ge(g_u, h + 1)
                if h:
                    v.wait_ge(g_o, h)
                V.tensor_copy(st[:, 0, :], B[3][:, 0:P]).then_inc(g_s, 1)
                for c in (1, 2):
                    v.wait_ge(g_s, 3 * h + c)
                    V.scalar_tensor_tensor(st[:, c, :], st[:, c - 1, :], xx[:, 1, c * P + P - 1:c * P + P],
                                           B[3][:, c * P:(c + 1) * P], op0=ALU.mult, op1=ALU.add).then_inc(g_s, 1)

            def biased(n, i, z, table, turned):
                v.wait_ge(z_ok, 4 * n + i + 1)
                if turned and i == 0:
                    v.wait_ge(t_ok, turned)
                c = 4 * (n % 2) + i
                if n >= 2:
                    v.wait_ge(e_ok, 4 * (n - 2) + i + 1)
                V.tensor_tensor_reduce(z[:, ZOFF[i]:ZOFF[i] + ZLEN[i]], B[4 + i][:, 0:ZLEN[i]],
                                       table[:, 384 - P * i:T], 1.0, -3.0e38, ALU.add, ALU.max,
                                       mxs[:, c:c + 1]).then_inc(zb_ok, 1)
                v.wait_ge(zb_ok, 4 * n + i + 1)
                V.tensor_scalar(nmx[:, c:c + 1], mxs[:, c:c + 1], -SCALE, None, ALU.mult).then_inc(m_ok, 1)

            dt = [0]

            def next_table(table, ratio):
                V.tensor_scalar(table[:], table[:], ratio, None, ALU.mult).then_inc(d_tab, 1)
                dt[0] += 1
                v.wait_ge(d_tab, dt[0])

            rr = [0]

            def rlink(ins):
                ins.then_inc(r_ok, 1)
                rr[0] += 1
                v.wait_ge(r_ok, rr[0])

            v.wait_ge(g_o, 4)
            for s in range(HEADS1 + 1):
                if s < HEADS1:
                    if s:
                        v.wait_ge(zb_ok, 8 * s)
                    next_table(dm1, 0.25)
                    for i in range(NT):
                        biased(2 * s, i, z1[:, 0], dm1, 4 * s)
                    for i in range(NT):
                        biased(2 * s + 1, i, z1[:, 1], dm1, 0)
                if s < HEADS1:
                    v.wait_ge(e_ok, 8 * (s + 1))
                    rlink(V.reciprocal(rcs, sums))
                    rlink(V.tensor_scalar(rcs[:, 4:8], rcs[:, 4:8], nlam, None, ALU.mult))
                    for i in range(NT):
                        a, b = (z1[:, m, ZOFF[i]:ZOFF[i] + ZLEN[i]] for m in range(2))
                        rlink(V.tensor_scalar(a, a, rcs[:, i:i + 1], None, ALU.mult))
                        V.scalar_tensor_tensor(a, b, rcs[:, 4 + i:5 + i], a, op0=ALU.mult, op1=ALU.add).then_inc(w_ok, 1)
                    v.wait_ge(w_ok, 4 * (s + 1))
                if s:
                    v.wait_ge(o_kept, s)
                    if s > 1:
                        v.wait_ge(ss_ok, 16 + 4 * (s - 1))
                    V.tensor_scalar(clamped[:], p1[:, 23 + s, :], CLAMP, -CLAMP, ALU.min,
                                    ALU.max).then_inc(o_clamped, 1)
            v.wait_ge(ss_ok, 32)
            V.tensor_scalar(okh, ssh, SQ_OVER, None, ALU.is_lt).then_inc(rs_ok, 1)
            v.wait_ge(rs_ok, 1)
            V.tensor_tensor(ssh, ssh, okh, ALU.mult).then_inc(rs_ok, 1)
            v.wait_ge(rs_ok, 3)
            rlink(V.reciprocal(rsh, rsh))
            rlink(V.tensor_tensor(rsh, rsh, okh, ALU.mult))
            for h in range(2 * HEADS1):
                o = p1[:, 8 + h, :] if h < HEADS1 else p1[:, 20 + h, :]
                V.tensor_tensor(o.rearrange("p (c d) -> p c d", c=NT), o.rearrange("p (c d) -> p c d", c=NT),
                                rsh[:, 4 * h:4 * h + 4].unsqueeze(2).broadcast_to([P, NT, P]),
                                ALU.mult).then_inc(mx_n, 1)
            for h in range(2 * HEADS1):
                v.wait_ge(mx_t, h + 1)
                if h >= 2:
                    v.wait_ge(mx_l, h - 1)
                m = z1[:, h % 2, 0:T]
                if h < HEADS1:
                    V.scalar_tensor_tensor(m, B[2 + h % 2][:], vt1[:, GNORM:GNORM + 1], p1[:, 12 + h, :],
                                           op0=ALU.mult, op1=ALU.mult).then_inc(mx_f, 1)
                else:
                    V.tensor_scalar(m, B[2 + h % 2][:], vt1[:, SUBLN:SUBLN + 1], 1.0 - LAMBDA_INIT,
                                    ALU.mult, ALU.mult).then_inc(mx_f, 1)
                v.wait_ge(mx_h, h + 1)
                V.tensor_tensor(mixl[:, h, :], m, mixh[:, h, :].bitcast(F32), ALU.subtract).then_inc(mx_l, 1)

            v.wait_ge(mod_out, 24)
            add_residual("out1", mod1[:, 16:24])
            norm_rstd(1)
            gains(1, mod1, vt1, NORM_B, 32)
            norm_u(1)
            ffn("ff1", 0)
            for s in (46, 47):
                v.wait_ge(ada_in, 16 * (s - 7))
                mod_products(1, ada, s)
            add_residual("down1", mod1[:, 40:48])
            norm_rstd(2)
            for t in range(KT):
                V.scalar_tensor_tensor(res[:, t, :], res[:, t, :], vt1[:, NORM_F + t:NORM_F + t + 1], rstd[:],
                                       op0=ALU.mult, op1=ALU.mult).then_inc(n_res, 1)
            v.wait_ge(n_res, KT)
            v.wait_ge(mod_out, 48)
            gains(2, mod2, vt2, NORM_A, 8)
            norm_rstd(3)
            norm_u(2)

            plain("qa2")
            ph = PH["kv2"]
            for c in range(7):
                ahead(ph, 0, c)
            plain("b2")
            V.memset(hc[:], 0.0).then_inc(c_hb, 1)
            v.wait_ge(c_hb, 1)
            v.wait_ge(c_in, 64)
            V.tensor_copy(w2c[:, 1, :], w2c[:, 0, :]).then_inc(c_hb, 1)
            for n in range(2):
                v.wait_ge(c_h, n + 1)
                V.tensor_copy(hb[:, n:n + 1], B[6 + n][:, 0:1]).then_inc(c_hb, 1)
                v.wait_ge(c_hb, n + 3)
                V.tensor_scalar(hx[:, n], B[4 + n][:, 0:GROUPS * NCMP], hb[:, n:n + 1], None,
                                ALU.add).then_inc(c_hx, 1)
            v.wait_ge(tab2, N_TAB2)
            v.wait_ge(c_z, 1)
            z3 = zc[:].rearrange("p i h n -> p (i h) n")
            for b in range(2):
                ins = V.tensor_tensor(zc[:, :, b:NSA_H:2, :],
                                      B[6 + b][:].rearrange("p (i h n) -> p i h n", i=NT, h=REP),
                                      bc[:, :, b:NSA_H:2, :], ALU.add)
                ins.then_inc(c_v, 1)
            v.wait_ge(c_v, 2)
            V.tensor_reduce(cmx, z3, AX_X, ALU.max).then_inc(c_v, 1)
            v.wait_ge(c_v, 3)
            V.tensor_tensor(z3, z3, cmx.unsqueeze(2).broadcast_to([P, 32, CPAD]), ALU.subtract).then_inc(c_v, 1)
            v.wait_ge(c_e, 1)
            cl = [1]

            def clink(ins):
                ins.then_inc(c_e, 1)
                cl[0] += 1
                v.wait_ge(c_e, cl[0])
            clink(V.tensor_reduce(csm, z3, AX_X, ALU.add))
            clink(V.reciprocal(csm, csm))
            v.wait_ge(v2_turned, 3)
            clink(V.tensor_tensor(csm.rearrange("p (i h) -> p i h", i=NT), csm.rearrange("p (i h) -> p i h", i=NT),
                                  gt[:, :, 0:24:3], ALU.mult))
            clink(V.tensor_tensor(csm.rearrange("p (i h) -> p i h", i=NT), csm.rearrange("p (i h) -> p i h", i=NT),
                                  rv.unsqueeze(2).broadcast_to([P, NT, NSA_H]), ALU.mult))
            clink(V.tensor_tensor(z3, z3, csm.unsqueeze(2).broadcast_to([P, 32, CPAD]), ALU.mult))
            v.wait_ge(c_t, 1)

            for s in range(8, 33):
                if s < 24:
                    if s % 2 == 0:
                        if s > 8:
                            v.wait_ge(zb_ok, 4 * s)
                        next_table(dm2, 0.5)
                    for i in range(NT):
                        biased(s, i, z2[:, s % 2], dm2, 4 * (s - 2 - 4) + 4 if s >= 10 else 0)
                elif s < 32:
                    for i in range(NT):
                        k = 4 * (s - 24) + i
                        v.wait_ge(z_ok, 4 * s + i + 1)
                        zd = B[4 + i][:, i * P:(i + 1) * P]
                        V.tensor_tensor(zd, zd, nst[:], ALU.add).then_inc(sb_m, 1)
                if s > 8 and s - 1 < 24:
                    n = s - 1
                    h, br = (n - 8) // 2, (n - 8) % 2
                    c0 = 4 * (n % 2)
                    v.wait_ge(e_ok, 4 * (n + 1))
                    rlink(V.reciprocal(rcs[:, c0:c0 + 4], sums[:, c0:c0 + 4]))
                    rlink(V.tensor_tensor(rcs[:, c0:c0 + 4], rcs[:, c0:c0 + 4], gt[:, :, 3 * h + 1 + br], ALU.mult))
                    for i in range(NT):
                        a = z2[:, n % 2, ZOFF[i]:ZOFF[i] + ZLEN[i]]
                        V.tensor_scalar(a, a, rcs[:, c0 + i:c0 + i + 1], None, ALU.mult).then_inc(w_ok, 1)
                elif s > 24:
                    n = s - 1
                    for i in range(NT):
                        k = 4 * (n - 24) + i
                        v.wait_ge(sb_s, 2 * (k + 1))
                        if k >= 2:
                            v.wait_ge(w_ok, 4 * (n - 4) + i - 1)
                        kp = z2[:, 0, ZOFF[i]:ZOFF[i] + ZLEN[i]]
                        sgm = z2[:, 1, ZOFF[i]:ZOFF[i] + ZLEN[i] - 1]
                        r = rb[:, k % 2, 0:ZLEN[i]]
                        V.tensor_tensor_scan(r[:, ::-1], kp[:, ::-1], kp[:, ::-1], 1.0, ALU.mult,
                                             ALU.bypass).then_inc(sb_r, 1)
                        v.wait_ge(sb_r, k + 1)
                        V.tensor_tensor(sgm, sgm, r[:, 1:ZLEN[i]], ALU.mult).then_inc(w_ok, 1)
                if s > 8:
                    n = s - 1
                    pair = (n - 8) // 4 if n < 24 else 4 + (n - 24) // 2
                    if (n < 24 and (n - 8) % 4 == 3) or (n >= 24 and n % 2 == 1):
                        v.wait_ge(mh_ok, pair + 1)
                        V.tensor_tensor(mil[:, pair, :], B[pair % 2][:], mih[:, pair, :].bitcast(F32),
                                        ALU.subtract).then_inc(ml_ok, 1)

            ph = PH["merge2"]

            def merge_body(i):
                for c in range(4):
                    ahead(ph, i, c)
                    if c >= 2:
                        b = c - 2
                        v.wait_ge(drain_a, i * 2 + (ph.a0 + b + 1))
                        v.wait_ge(unit_done, i * 4 + (ph.u0 + c + 1) + U1)
                        V.tensor_tensor(ms[:, b], ms[:, b], B[c][:], ALU.mult).then_inc(drain_v, 1)
                v.wait_ge(drain_v, i * 2 + (ph.d0 + 2))
                V.tensor_tensor(yf[:, 0], ms[:, 0], ms[:, 1], ALU.add).then_inc(y_f, 1)
                v.wait_ge(y_h, i + 1)
                ysl = yl[:, ds(i, 1), :].rearrange("p a t -> p (a t)")
                V.tensor_tensor(ysl, yf[:, 0], yh[:, ds(i, 1), :].rearrange("p a t -> p (a t)").bitcast(F32),
                                ALU.subtract).then_inc(y_l, 1)
            loop(ph, merge_body)
            add_residual("out2", mod2[:, 16:24])
            norm_rstd(4)
            gains(3, mod2, vt2, NORM_B, 32)
            norm_u(3)
            ffn("ff2", FT)
            add_residual("down2", mod2[:, 40:48], skip_last=True)
            norm_rstd(5)
            for k in range(KT):
                if k >= 2:
                    v.wait_ge(o_t, k - 1)
                V.scalar_tensor_tensor(onorm[:, k % 2], res[:, k, :], vt2[:, NORM_F + k:NORM_F + k + 1], rstd[:],
                                       op0=ALU.mult, op1=ALU.mult).then_inc(o_n, 1)


_INS = [
    "x", "c", "w_ada", "b_ada", "norm1_w", "w_in", "hgrn_lb_logits", "hgrn_gnorm_w", "diff_lambda_q1",
    "diff_lambda_k1", "diff_lambda_q2", "diff_lambda_k2", "diff_subln_w", "w_out", "norm2_w", "w_ffn_gate",
    "w_ffn_up", "w_ffn_down", "final_norm_w", "c_2", "w_ada_2", "b_ada_2", "norm_mix_g_2", "w_in_2",
    "cmp_pos_k_2", "cmp_w1_k_2", "cmp_w2_k_2", "cmp_pos_v_2", "cmp_w1_v_2", "cmp_w2_v_2", "w_proj_a_2",
    "w_proj_b_2", "w_out_2", "norm_ffn_g_2", "w_ffn_gate_2", "w_ffn_up_2", "w_ffn_down_2", "norm_final_g_2",
]


def kernel(**inputs):
    import numpy as _np
    import concourse.bacc as _bacc
    from concourse import mybir as _mybir
    from concourse.bass_utils import run_bass_kernel_spmd as _run

    nc = _bacc.Bacc("TRN2", target_bir_lowering=False, num_devices=1)
    arrays, t_in = {}, {}
    for name in _INS:
        a = _np.ascontiguousarray(inputs[name])
        arrays[f"in_{name}_dram"] = a
        t_in[name] = nc.dram_tensor(f"in_{name}_dram", a.shape, _mybir.dt.from_np(a.dtype), kind="ExternalInput").ap()
    out = nc.dram_tensor("out_0_dram", (1, T, D), F32, kind="ExternalOutput").ap()
    build(nc, t_in, out)
    r = _run(nc, [arrays], core_ids=[0])
    return r.results[0]["out_0_dram"]
```

```python
from contextlib import ExitStack

import concourse.bass as bass
from concourse import mybir

F32 = mybir.dt.float32
F32R = mybir.dt.float32r
I32 = mybir.dt.int32
ALU = mybir.AluOpType
ACT = mybir.ActivationFunctionType
AX_X = mybir.AxisListType.X
ds = bass.ds

P = 128
T = 512
NT = T // P
D = 1024
KT = D // P
F = 2816
FT = F // P
HEADS1 = 4
NSA_H, GROUPS, REP, HD = 8, 2, 4, 64
NCMP, CPAD, CSTRIDE, CBLOCK = 31, 32, 16, 32
EPS = 1e-6
BIG = -1.0e30
SCALE = HD ** -0.5
INV = 1.0 / SCALE
LAMBDA_INIT = 0.2
MODC = 256
LEVELS = [64, 32, 16, 8, 4, 2, 1]
ZOFF = [0, 128, 384, 768]
ZLEN = [P * (i + 1) for i in range(NT)]
ZW = sum(ZLEN)

CLAMP, SQ_SCALE, SQ_BACK, SQ_OVER = 2.0 ** 64, 2.0 ** -34, 2.0 ** 68, 2.0 ** 60

B_ADA, NORM_A, NORM_B, NORM_F, LB, GNORM, SUBLN = 0, 48, 56, 64, 72, 80, 81
POS_K, POS_V = 72, 88
U1, H1, Y1 = 1, 1, 1


class Phase:

    def __init__(self, name, iters, units, act, dve):
        self.name, self.iters, self.units, self.act, self.dve = name, iters, units, act, dve


def plan():
    order = [
        Phase("q1", 2, 2, 2, 0), Phase("f1", 2, 2, 2, 0), Phase("i1", 2, 2, 2, 0),
        Phase("g1", 2, 2, 2, 0), Phase("a1", 6, 2, 2, 0),
        Phase("out1", 4, 2, 0, 2), Phase("ff1", 22, 2, 1, 0), Phase("down1", 4, 6, 0, 2),
        Phase("qa2", 2, 2, 2, 0), Phase("kv2", 1, 7, 7, 0), Phase("b2", 6, 2, 2, 0),
        Phase("merge2", 8, 4, 2, 2),
        Phase("out2", 4, 2, 0, 2), Phase("ff2", 22, 2, 1, 0), Phase("down2", 4, 6, 0, 2),
    ]
    u, a, d = 0, KT, 2
    for ph in order:
        ph.u0, ph.a0, ph.d0 = u, a, d
        u, a, d = u + ph.iters * ph.units, a + ph.iters * ph.act, d + ph.iters * ph.dve
    return {ph.name: ph for ph in order}, u


def build(nc, t_in, out):
    PH, UNITS = plan()
    ctx = ExitStack()
    with ctx:
        base = 16640
        here = [base]

        def at(name, shape, dt=F32, where=None):
            n = 4
            for s in shape[1:]:
                n *= s
            off = here[0] if where is None else where
            if where is None:
                here[0] += (n + 31) // 32 * 32
            return nc.alloc_sbuf_tensor_at(name, shape, dt, offset=off)

        res = at("res", [P, KT, T])
        u_at = here[0]
        uh = at("uh", [P, KT, T], F32R)
        ul = at("ul", [P, KT, T], F32R)
        wraw = at("wraw", [P, 2, KT * P])
        wh = at("wh", [P, 2, KT * P], F32R)
        wl = at("wl", [P, 2, KT * P], F32R)
        a_at = here[0]
        ada = at("ada", [P, KT, MODC])
        acc = at("acc", [P, MODC])
        ident = at("ident", [P, P])
        ones = at("ones", [P, P])
        vt1 = at("vt1", [P, P])
        vt2 = at("vt2", [P, P])
        mod1 = at("mod1", [P, 48])
        mod2 = at("mod2", [P, 48])
        gain = at("gain", [P, 4, KT])
        sc_c = at("sc_c", [P, 2, KT])
        ct = at("ct", [P, 2, KT])
        lamv = at("lamv", [P, 4, HD])
        tiny = at("tiny", [P, 64])
        n_at = here[0]
        ssq = at("ssq", [P, T])
        sq = at("sq", [P, 2, T])
        rstd = at("rstd", [P, T])
        tn = at("tn", [P, 2, T])
        u32 = at("u32", [P, 2, T])
        r_at = here[0]
        K2 = 4 * T

        xin = at("xin", [P, NT, D], where=r_at)
        ada0 = at("ada0", [P, 8, KT, MODC], where=r_at + 8 * K2)
        V_CHUNKS = 6
        acc0 = at("acc0", [P, V_CHUNKS, MODC], where=u_at)
        v1 = at("v1", [P, P], where=r_at + 8 * K2 + 32 * K2)
        v2 = at("v2", [P, P], where=r_at + 8 * K2 + 32 * K2 + 512)
        p1 = at("p1", [P, 28, T], where=r_at)
        mixh = at("mixh", [P, KT, T], F32R, where=r_at + 28 * K2)
        mixl = at("mixl", [P, KT, T], F32R, where=r_at + 36 * K2)
        s_at = r_at + 44 * K2
        h_at = r_at + 28 * K2
        bb = at("bb", [P, T], where=h_at)
        xx = at("xx", [P, 2, T], where=h_at + 1 * K2)
        ql = at("ql", [P, 2, T], where=h_at + 3 * K2)
        kl = at("kl", [P, 2, T], where=h_at + 5 * K2)
        am = at("am", [P, T], where=h_at + 7 * K2)
        q0 = at("q0", [P, T], where=h_at + 8 * K2)
        kht = at("kht", [P, T], where=h_at + 9 * K2)
        vtm = at("vtm", [P, T], where=h_at + 10 * K2)
        st = at("st", [P, 3, P], where=h_at + 11 * K2)
        ff = at("ff", [P, T], where=h_at + 12 * K2)
        rmask = at("rmask", [P, T], where=n_at + 6 * K2)
        lmask = at("lmask", [P, 8, P], I32, where=n_at + 3 * K2)
        scrap = at("scrap", [P, 4, P], I32, where=n_at + 7 * K2)
        junk = at("junk", [P, T], where=h_at + 13 * K2)
        z1 = at("z1", [P, 2, ZW], where=s_at)
        dm1 = at("dm1", [P, T], where=n_at + 2 * K2 + K2 * 3)
        wt1 = at("wt1", [P, 2, NT, T], where=u_at)
        vd1 = at("vd1", [P, 2, T], where=u_at + 8 * K2)
        junk1 = at("junk1", [P, T], where=u_at + 10 * K2)
        clamped = at("clamped", [P, T], where=u_at + 11 * K2)
        hh = at("hh", [P, FT, T], F32R, where=r_at)
        hl = at("hl", [P, FT, T], F32R, where=r_at + FT * K2)
        sg = at("sg", [P, 2, T], where=r_at + 2 * FT * K2)
        hf = at("hf", [P, 2, T], where=r_at + 2 * FT * K2 + 2 * K2)
        qa = at("qa", [P, 4, T], where=r_at)
        kdup = at("kdup", [P, 2, GROUPS, T], where=r_at + 4 * K2)
        qkvb = at("qkvb", [P, 12, T], where=r_at + 8 * K2)
        vsw = at("vsw", [P, 2, T], where=r_at + 20 * K2)
        vbt = at("vbt", [P, 4, T], where=r_at + 22 * K2)
        wct = at("wct", [P, GROUPS, T], where=r_at + 26 * K2)
        mih = at("mih", [P, KT, T], F32R, where=r_at + 28 * K2)
        mil = at("mil", [P, KT, T], F32R, where=r_at + 36 * K2)
        w1c = at("w1c", [P, 2, 16, P], where=r_at + 28 * K2)
        kds = at("kds", [P, 2, GROUPS, T], where=r_at + 36 * K2)
        vswT = at("vswT", [P, 2, T], where=r_at + 40 * K2)
        gateT = at("gateT", [P, T], where=r_at + 42 * K2)
        zc = at("zc", [P, NT, NSA_H, CPAD], where=s_at)
        w2c = at("w2c", [P, 3, HD], where=s_at + 2 * K2)
        hc = at("hc", [P, 2, GROUPS, CPAD], where=s_at + 3 * K2)
        hcr = at("hcr", [P, GROUPS, REP, CPAD], where=s_at + 3 * K2 + 512)
        hx = at("hx", [P, 2, GROUPS * NCMP], where=s_at + 4 * K2)
        z2 = at("z2", [P, 2, ZW], where=s_at)
        wt2 = at("wt2", [P, NT, T], where=s_at + 5 * K2)
        kc = at("kc", [P, GROUPS, CPAD], where=a_at)
        vc = at("vc", [P, GROUPS, HD], where=a_at + 256)
        gt = at("gt", [P, NT, 24], where=a_at + 768)
        bc = at("bc", [P, NT, NSA_H, CPAD], where=n_at)
        dc = at("dc", [P, NT, CPAD], where=n_at + 2 * K2)
        dm2 = at("dm2", [P, T], where=n_at + 3 * K2)
        rb = at("rb", [P, 2, T], where=n_at + 4 * K2)
        nst = at("nst", [P, P], where=n_at + 6 * K2)
        yh = at("yh", [P, KT, T], F32R, where=r_at)
        yl = at("yl", [P, KT, T], F32R, where=r_at + 8 * K2)
        ms = at("ms", [P, 2, T], where=r_at + 16 * K2)
        yf = at("yf", [P, 2, T], where=r_at + 18 * K2)
        onorm = at("onorm", [P, 2, T], where=r_at)
        outb = at("outb", [P, NT, D], where=r_at + 2 * K2)

        sm = at("sm", [P, 160], where=s_at + 9 * K2)
        mxs, nmx, sums, rcs = sm[:, 0:8], sm[:, 8:16], sm[:, 16:24], sm[:, 24:32]
        ssh = sm[:, 32:64]
        rsh = sm[:, 64:96]
        cmx, csm = sm[:, 96:128], sm[:, 128:160]
        okh = cmx
        hb = tiny[:, 48:50]
        lbs, oml = tiny[:, 0:4], tiny[:, 4:8]
        nlam = tiny[:, 8:9]
        lsc = tiny[:, 10:34]
        rv = tiny[:, 40:44]
        epst = tiny[:, 44:45]

        B = [ctx.enter_context(nc.psum_tensor(f"bank{i}", [P, T], F32)) for i in range(8)]

        def sem(name):
            return ctx.enter_context(nc.semaphore(name))

        x_in, vec_in, ada0_in = sem("x_in"), sem("vec_in"), [sem(f"ada0_in{i}") for i in range(8)]
        ct_in = sem("ct_in")
        const_ok, zeroed, vecT, vecT_out = sem("const_ok"), sem("zeroed"), sem("vecT"), sem("vecT_out")
        setup_v, setup_a = sem("setup_v"), sem("setup_a")
        w_in = [sem("w_in0"), sem("w_in1")]
        w_hi, w_split = sem("w_hi"), sem("w_split")
        unit_done = sem("unit_done")
        drain_a, drain_v = sem("drain_a"), sem("drain_v")
        ada_lo_in, mod_step, mod_acc = sem("ada_lo_in"), sem("mod_step"), sem("mod_acc")
        mod_tree_ok = sem("mod_tree_ok")
        ada_hi_in = sem("ada_hi_in")
        mod_sum, mod_out = sem("mod_sum"), sem("mod_out")
        x_turned = sem("x_turned")
        sq_ok, ssq_ok = sem("sq_ok"), sem("ssq_ok")
        n_sum, n_std, n_rstd = sem("n_sum"), sem("n_std"), sem("n_rstd")
        gain_ok = sem("gain_ok")
        n_t, n_u32, n_uh, n_ul = sem("n_t"), sem("n_u32"), sem("n_uh"), sem("n_ul")
        n_res = sem("n_res")
        silu_ok, h_ok, hh_ok, hl_ok = sem("silu_ok"), sem("h_ok"), sem("hh_ok"), sem("hl_ok")
        g_f, g_k, g_ln, g_bb = sem("g_f"), sem("g_k"), sem("g_ln"), sem("g_bb")
        g_x, g_e, g_qk, g_p, g_a = sem("g_x"), sem("g_e"), sem("g_qk"), sem("g_p"), sem("g_a")
        g_q0, g_kh, g_turn, g_turned = sem("g_q0"), sem("g_kh"), sem("g_turn"), sem("g_turned")
        g_u, g_s, g_o = sem("g_u"), sem("g_s"), sem("g_o")
        g_zero, g_cleared = sem("g_zero"), sem("g_cleared")
        ss_ok, rs_ok, o_kept, o_clamped = sem("ss_ok"), sem("rs_ok"), sem("o_kept"), sem("o_clamped")
        mx_n, mx_t, mx_f, mx_h, mx_l = sem("mx_n"), sem("mx_t"), sem("mx_f"), sem("mx_h"), sem("mx_l")
        d_tab, z_ok, zb_ok, m_ok, e_ok = sem("d_tab"), sem("z_ok"), sem("zb_ok"), sem("m_ok"), sem("e_ok")
        r_ok, w_ok, t_ok, wt_ok, pv_ok = sem("r_ok"), sem("w_ok"), sem("t_ok"), sem("wt_ok"), sem("pv_ok")
        v_turn, v_turned = sem("v_turn"), sem("v_turned")
        sb_m, sb_s, sb_r = sem("sb_m"), sem("sb_s"), sem("sb_r")
        pair_ok, mh_ok, ml_ok = sem("pair_ok"), sem("mh_ok"), sem("ml_ok")
        c_in, tab2, c_h, c_hb, c_hx, c_hg = (sem("c_in"), sem("tab2"), sem("c_h"), sem("c_hb"), sem("c_hx"), sem("c_hg"))
        c_kv, c_kvc = sem("c_kv"), sem("c_kvc")
        c_z, c_v, c_e, c_t, c_wt = sem("c_z"), sem("c_v"), sem("c_e"), sem("c_t"), sem("c_wt")
        v2_turn, v2_turned = sem("v2_turn"), sem("v2_turned")
        y_f, y_h, y_l = sem("y_f"), sem("y_h"), sem("y_l")
        o_n, o_t, o_c, stored = sem("o_n"), sem("o_t"), sem("o_c"), sem("stored")

        block = ctx.enter_context(nc.Block())

        def wview(name):
            return t_in[name][0].rearrange("(k p) f -> p k f", p=P)

        W = {n: wview(n) for n in ("w_in", "w_out", "w_ffn_gate", "w_ffn_up", "w_ffn_down", "w_in_2",
                                   "w_proj_a_2", "w_proj_b_2", "w_out_2", "w_ffn_gate_2", "w_ffn_up_2",
                                   "w_ffn_down_2")}
        ADA = [t_in[n][0].rearrange("(p k) f -> p k f", k=KT) for n in ("w_ada", "w_ada_2")]
        DOWN = [(0, 8), (8, 16), (16, 22)]

        def unit_source(name, i, c, snap):
            def ds(first, n):
                return bass.ds(first if isinstance(first, int) else snap(first), n)

            col0 = {"q1": 0, "f1": 512, "i1": 1024, "g1": 1536, "a1": 2048}
            if name in col0:
                return W["w_in"][:, :, ds(i * 256 + (col0[name] + c * P), P)], KT, P
            if name in ("out1", "out2"):
                w = W["w_out" if name == "out1" else "w_out_2"]
                return w[:, :, ds(i * 256 + c * P, P)], KT, P
            if name in ("ff1", "ff2"):
                w = W[("w_ffn_gate", "w_ffn_up")[c] + ("" if name == "ff1" else "_2")]
                return w[:, :, ds(i * P, P)], KT, P
            if name in ("down1", "down2"):
                a, b = DOWN[c % 3]
                w = W["w_ffn_down" if name == "down1" else "w_ffn_down_2"]
                return w[:, a:b, ds(i * 256 + (c // 3) * P, P)], b - a, P
            if name == "qa2":
                return W["w_in_2"][:, :, ds(i * 256 + c * P, P)], KT, P
            if name == "kv2":
                n = P if c < 6 else 24
                return W["w_in_2"][:, :, 512 + c * P:512 + c * P + n], KT, n
            if name == "b2":
                return W["w_in_2"][:, :, ds(i * 256 + (1304 + c * P), P)], KT, P
            if c < 2:
                return W["w_in_2"][:, :, ds(i * P + (2840 + c * D), P)], KT, P
            return W[("w_proj_a_2", "w_proj_b_2")[c - 2]][:, :, ds(i * P, P)], 4, P

        RIDE = {"q1": [(0, 2, 0, 8)], "f1": [(0, 2, 0, 10)], "i1": [(0, 2, 0, 12)], "g1": [(0, 2, 0, 14)],
                "a1": [(0, 6, 0, 16)], "ff1": [(0, 2, 0, 22), (2, 22, 1, -2)], "down1": [(0, 4, 1, 20)]}
        MOD0 = {"q1": 8, "f1": 10, "i1": 12, "g1": 14, "a1": 16, "ff1": 22, "down1": 44}

        A1_UNITS, SLOTS = 12, 8 * HEADS1
        PER_SLOT = A1_UNITS * KT // SLOTS
        DRAIN_AT = {(KT * n + KT - 1) // PER_SLOT + 2: n for n in range(A1_UNITS)}
        SPLIT_AT = {(KT * n - 1) // PER_SLOT + 1: n for n in range(A1_UNITS)}
        MOD_AT = {4: 16, 10: 17, 14: 18, 19: 19, 22: 20, 29: 21}

        def runs(name, peel=False, part=None):
            out_ = []
            for a, b, m, c0 in RIDE.get(name, [(*(part or (0, PH[name].iters)), None, 0)]):
                if peel and a == 0:
                    out_.append((0, 1, m, c0))
                    a = 1
                if a < b:
                    out_.append((a, b, m, c0))
            return out_

        def over(eng, name, body, peel=False, part=None):
            for a, b, m, c0 in runs(name, peel, part):
                if b == a + 1:
                    body(a, m, a + c0)
                else:
                    with eng.Fori(a, b) as i:
                        body(i, m, i + c0)

        @block.sync
        def _(sp):
            def load_unit(ph, i, c):
                u = i * ph.units + (ph.u0 + c)
                slot = (ph.u0 + c) % 2 if ph.units % 2 == 0 else (ph.u0 + c) % 2
                src, nk, n = unit_source(ph.name, i, c, sp.snap)
                dst = wraw[:, slot, 0:nk * P].rearrange("p (k f) -> p k f", k=nk)[:, :, 0:n]
                if ph.name == "merge2" and c == 1:
                    sp.wait_ge(w_split, u)
                elif not (isinstance(u, int) and u < 2) and not (ph.name == "merge2" and c == 2):
                    sp.wait_ge(w_split, u - 1)
                sp.dma_start(dst, src).then_inc(w_in[slot], 16)

            def load_ada(m, chunk, step):
                if isinstance(chunk, int):
                    first, second = chunk * MODC, chunk * MODC + P
                else:
                    first, second = sp.snap(chunk * MODC), sp.snap(chunk * MODC + P)
                if not (isinstance(step, int) and step == 8):
                    sp.wait_ge(mod_tree_ok, step * 7 - 7 * 9 + 4)
                sp.dma_start(ada[:, :, 0:P], ADA[m][:, :, ds(first, P)]).then_inc(ada_lo_in, 16)
                sp.wait_ge(mod_acc, step)
                sp.dma_start(ada[:, :, P:MODC], ADA[m][:, :, ds(second, P)]).then_inc(ada_hi_in, 16)

            sp.dma_start(ct[:, 0, :], t_in["c"][0].rearrange("(p k) -> p k", k=KT)).then_inc(ct_in, 16)
            sp.dma_start(ct[:, 1, :], t_in["c_2"][0].rearrange("(p k) -> p k", k=KT)).then_inc(ct_in, 16)
            sp.dma_start(xin[:], t_in["x"][0].rearrange("(j p) d -> p j d", p=P)).then_inc(x_in, 16)
            for c in range(8):
                sp.dma_start(ada0[:, c], ADA[0][:, :, c * MODC:(c + 1) * MODC]).then_inc(ada0_in[c], 16)

            def gemm(name, tail=None):
                ph = PH[name]

                def body(i, m, chunk):
                    for c in range(ph.units):
                        load_unit(ph, i, c)
                        if c == 1 and tail and isinstance(i, int) and i == 0:
                            tail()
                    if m is not None:
                        load_ada(m, chunk, i + MOD0[name])
                over(sp, name, body, peel=bool(tail) or ph.u0 == 0)

            for name in ("q1", "f1", "i1", "g1", "a1"):
                gemm(name)

            def compress_weights():
                sp.wait_ge(n_res, KT)
                for n, (w1, w2) in enumerate((("cmp_w1_k_2", "cmp_w2_k_2"), ("cmp_w1_v_2", "cmp_w2_v_2"))):
                    sp.dma_start(w1c[:, n], t_in[w1][0].rearrange("(j p) h -> p j h", p=P)).then_inc(c_in, 16)
                    sp.dma_start(w2c[:, 2 * n, :], t_in[w2][0]).then_inc(c_in, 16)

            gemm("out1")
            gemm("ff1")
            gemm("down1")
            gemm("qa2", tail=compress_weights)
            gemm("kv2")
            gemm("b2")
            gemm("merge2")
            gemm("out2")
            gemm("ff2")
            gemm("down2")
            sp.wait_ge(o_c, KT)
            sp.dma_start(out[0].rearrange("(j p) d -> p j d", p=P), outb[:]).then_inc(stored, 16)
            sp.wait_ge(stored, 16)

        @block.gpsimd
        def _(g):
            n = [0]

            def step(ins, signal=const_ok):
                ins.then_inc(signal, 1)
                n[0] += 1
                g.wait_ge(signal, n[0])

            nc.gpsimd.memset(v1[:], 0.0).then_inc(zeroed, 1)
            nc.gpsimd.memset(v2[:], 0.0).then_inc(zeroed, 1)
            step(nc.gpsimd.memset(ident[:], 0.0))
            step(nc.gpsimd.affine_select(out=ident[:], in_=ident[:], compare_op=ALU.not_equal, fill=1.0, base=0,
                                         pattern=[[-1, P]], channel_multiplier=1))
            step(nc.gpsimd.memset(ones[:], 1.0))
            step(nc.gpsimd.memset(epst, EPS))

            def sum_squares(k):
                if k:
                    g.wait_ge(n_sum, k)
                nc.gpsimd.memset(ssq[:], 0.0).then_inc(ssq_ok, 1)
                for t in range(KT):
                    g.wait_ge(sq_ok, KT * k + t + 1)
                    g.wait_ge(ssq_ok, 9 * k + t + 1)
                    nc.gpsimd.tensor_tensor(ssq[:], ssq[:], sq[:, t % 2], ALU.add).then_inc(ssq_ok, 1)

            def mod_tree(m, step):
                for c, landed in enumerate((ada_lo_in, ada_hi_in)):
                    n0 = step * 7 - 7 * 8 + 4 * c
                    cc = slice(c * P, (c + 1) * P)
                    g.wait_ge(landed, step * 16 - 16 * 7)
                    nc.gpsimd.tensor_tensor(ada[:, :, cc], ada[:, :, cc],
                                            sc_c[:, m, :].unsqueeze(2).broadcast_to([P, KT, P]),
                                            ALU.mult).then_inc(mod_tree_ok, 1)
                    for k, n in ((4, 1), (2, 2)):
                        g.wait_ge(mod_tree_ok, n0 + n)
                        nc.gpsimd.tensor_tensor(ada[:, 0:k, cc], ada[:, 0:k, cc], ada[:, k:2 * k, cc],
                                                ALU.add).then_inc(mod_tree_ok, 1)
                    g.wait_ge(mod_tree_ok, n0 + 3)
                    if c == 0:
                        g.wait_ge(mod_sum, step)
                    nc.gpsimd.tensor_tensor(acc[:, cc], ada[:, 0, cc], ada[:, 1, cc],
                                            ALU.add).then_inc(mod_acc if c else mod_tree_ok, 1)

            def ride(name):
                over(g, name, lambda i, m, chunk: mod_tree(m, i + MOD0[name]))

            sum_squares(0)
            ride("q1")
            g.wait_ge(n_ul, KT)
            step(nc.gpsimd.iota(lmask[:, 7, :], [[1, P]], base=0, channel_multiplier=0))
            step(nc.gpsimd.iota(lmask[:, 6, :], [[0, P]], base=0, channel_multiplier=1))
            step(nc.gpsimd.memset(rmask[:], 1.0))
            step(nc.gpsimd.memset(rmask[:, 0:T:P], 0.0))
            for tile_ in (ql, kl, am):
                nc.gpsimd.memset(tile_[:], 0.0).then_inc(g_cleared, 1)
            for name in ("f1", "i1", "g1", "a1"):
                ride(name)
            step(nc.gpsimd.iota(dm1[:], [[8, T]], base=-8 * 384, channel_multiplier=-8,
                                allow_small_or_imprecise_dtypes=True))
            step(nc.gpsimd.affine_select(out=dm1[:], in_=dm1[:], compare_op=ALU.is_ge, fill=BIG, base=384,
                                         pattern=[[-1, T]], channel_multiplier=1))
            g.wait_ge(mx_l, KT)
            sum_squares(1)
            ride("ff1")
            g.wait_ge(n_sum, 2)
            nc.gpsimd.memset(ssq[:], 0.0).then_inc(ssq_ok, 1)

            def down_body(i, m, chunk):
                mod_tree(m, i + MOD0["down1"])
                for c in range(2):
                    g.wait_ge(sq_ok, i * 2 + (KT * 2 + c + 1))
                    g.wait_ge(ssq_ok, i * 2 + (9 * 2 + c + 1))
                    nc.gpsimd.tensor_tensor(ssq[:], ssq[:], sq[:, c], ALU.add).then_inc(ssq_ok, 1)
            over(g, "down1", down_body)
            sum_squares(3)
            g.wait_ge(n_ul, KT * 3)
            m = [0]

            def step2(ins):
                ins.then_inc(tab2, 1)
                m[0] += 1
                g.wait_ge(tab2, m[0])

            step2(nc.gpsimd.iota(dc[:], [[-8 * P, NT], [8 * CSTRIDE, CPAD]], base=8 * (CBLOCK - 1),
                                 channel_multiplier=-8, allow_small_or_imprecise_dtypes=True))
            step2(nc.gpsimd.affine_select(out=dc[:], in_=dc[:], compare_op=ALU.is_ge, fill=BIG, base=-(CBLOCK - 1),
                                          pattern=[[P, NT], [-CSTRIDE, CPAD]], channel_multiplier=1))
            for h in range(NSA_H):
                step2(nc.gpsimd.tensor_scalar(bc[:, :, h, :], dc[:], 2.0 ** -(h + 1), None, ALU.mult))
            step2(nc.gpsimd.memset(rv, 1.0))
            step2(nc.gpsimd.affine_select(out=rv[:, 0:1], in_=rv[:, 0:1], compare_op=ALU.is_ge, fill=0.0,
                                          base=-(CBLOCK - 1), pattern=[[0, 1]], channel_multiplier=1))
            step2(nc.gpsimd.iota(dm2[:], [[8, T]], base=-8 * 384, channel_multiplier=-8,
                                 allow_small_or_imprecise_dtypes=True))
            step2(nc.gpsimd.affine_select(out=dm2[:], in_=dm2[:], compare_op=ALU.is_ge, fill=BIG, base=384,
                                          pattern=[[-1, T]], channel_multiplier=1))
            step2(nc.gpsimd.memset(nst[:], 0.0))
            step2(nc.gpsimd.affine_select(out=nst[:], in_=nst[:], compare_op=ALU.is_ge, fill=BIG, base=-1,
                                          pattern=[[-1, P]], channel_multiplier=1))
            g.wait_ge(ml_ok, 8)
            sum_squares(4)
            sum_squares(5)

        N_TAB2 = 2 + NSA_H + 2 + 2 + 2

        @block.tensor
        def _(pe):
            def passes(bank, slot, nk, rh, rl, k0, first, last, tiles=None):
                for k in range(nk):
                    if tiles is not None:
                        pe.wait_ge(tiles[0], tiles[1] + k + 1)
                    a = wh[:, slot, k * P:(k + 1) * P]
                    b = wl[:, slot, k * P:(k + 1) * P]
                    nc.tensor.matmul(bank[:], a, rh[:, k0 + k, :], start=(first and k == 0), stop=False)
                    nc.tensor.matmul(bank[:], a, rl[:, k0 + k, :], start=False, stop=False)
                    mm = nc.tensor.matmul(bank[:], b, rh[:, k0 + k, :], start=False, stop=(last and k == nk - 1))
                mm.then_inc(unit_done, 1)

            def take(ph, i, c):
                pe.wait_ge(w_split, i * ph.units + (ph.u0 + c + 1))
                return (ph.u0 + c) % 2

            def mod_sums(step, col, bank=B[5], acc=acc[:]):
                pe.wait_ge(mod_acc, step + 1)
                for half in range(2):
                    mm = nc.tensor.matmul(bank[:, col + half:col + half + 1], acc[:, half * P:(half + 1) * P],
                                          ones[:, 0:1], start=True, stop=True)
                mm.then_inc(mod_sum, 1)

            def mod_matmuls(step, bank=B[5]):
                pe.wait_ge(mod_out, step)
                mod_sums(step, 0, bank)

            def simple(name, rh, rl, n_before=None, part=None):
                ph = PH[name]

                def body(i, m, chunk):
                    for c in range(2):
                        slot = take(ph, i, c)
                        pe.wait_ge(drain_a, i * 2 + (ph.a0 + c - 1))
                        first = n_before is not None and c == 0 and isinstance(i, int) and i == 0
                        passes(B[(ph.u0 + c) % 2], slot, KT, rh, rl, 0, True, True,
                               (n_ul, n_before) if first else None)
                    if m is not None:
                        mod_matmuls(i + MOD0[name])
                over(pe, name, body, peel=n_before is not None, part=part)

            def out_proj(name, rh, rl, ready):
                ph = PH[name]

                def body(i, m, chunk):
                    for c in range(2):
                        slot = take(ph, i, c)
                        pe.wait_ge(drain_v, i * 2 + (ph.d0 + c - 1))
                        first = c == 0 and isinstance(i, int) and i == 0
                        if first:
                            pe.wait_ge(drain_a, ph.a0)
                        passes(B[c], slot, KT, rh, rl, 0, True, True, ready if first else None)
                over(pe, name, body, peel=True)

            def ffn(name, n_before, h0):
                ph = PH[name]

                def body(i, m, chunk):
                    first = isinstance(i, int) and i == 0
                    slot = take(ph, i, 0)
                    pe.wait_ge(drain_a, i + ph.a0)
                    passes(B[0], slot, KT, uh, ul, 0, True, True, (n_ul, n_before) if first else None)
                    slot = take(ph, i, 1)
                    pe.wait_ge(h_ok, i + h0)
                    passes(B[1], slot, KT, uh, ul, 0, True, True)
                    if m is not None:
                        mod_matmuls(i + MOD0[name])
                over(pe, name, body, peel=True)

            def down(name, h_before):
                ph = PH[name]

                def body(i, m, chunk):
                    first = isinstance(i, int) and i == 0
                    for t in range(2):
                        pe.wait_ge(drain_v, i * 2 + (ph.d0 + t - 1))
                        if first and t == 0:
                            pe.wait_ge(drain_a, ph.a0)
                        for c, (a, b) in enumerate(DOWN):
                            slot = take(ph, i, 3 * t + c)
                            passes(B[t], slot, b - a, hh, hl, a, c == 0, c == 2,
                                   (hl_ok, h_before + a) if first and t == 0 else None)
                    if m is not None:
                        mod_matmuls(i + MOD0[name])
                over(pe, name, body, peel=True)

            def norm(k):
                pe.wait_ge(ssq_ok, 9 * (k + 1))
                nc.tensor.matmul(B[4][:], ones[:], ssq[:], start=True, stop=True).then_inc(n_sum, 1)

            pe.wait_ge(const_ok, 4)
            pe.wait_ge(setup_a, 1)
            pe.wait_ge(x_in, 16)
            for k in range(KT):
                if k >= 2:
                    pe.wait_ge(drain_a, k - 1)
                for j in range(NT):
                    mm = nc.tensor.transpose(B[k % 2][:, j * P:(j + 1) * P], xin[:, j, k * P:(k + 1) * P], ident[:])
                mm.then_inc(x_turned, 1)
            norm(0)
            for s in range(V_CHUNKS, 8):
                pe.wait_ge(ada0_in[s], 16)
                for half in range(2):
                    col = 2 * s + half
                    for k in range(KT):
                        mm = nc.tensor.matmul(B[5][:, col:col + 1], ada0[:, s, k, half * P:(half + 1) * P],
                                              sc_c[:, 0, k:k + 1], start=(k == 0), stop=(k == KT - 1))
                mm.then_inc(mod_sum, 1)
            for s in range(V_CHUNKS):
                mod_sums(s, 2 * s, acc=acc0[:, s])
            pe.wait_ge(vec_in, 16 * 17)
            nc.tensor.transpose(B[6][:, 0:P], v1[:], ident[:]).then_inc(unit_done, U1)
            nc.tensor.transpose(B[6][:, P:2 * P], v2[:], ident[:]).then_inc(vecT, 1)
            for name in ("q1", "f1", "i1", "g1"):
                simple(name, uh, ul, 0 if name == "q1" else None)
            pe.wait_ge(drain_a, PH["a1"].a0)

            def a1_slot(p):
                ph = PH["a1"]
                for n, k in (divmod(x, KT) for x in range(PER_SLOT * p, PER_SLOT * (p + 1))):
                    if k == 0:
                        take(ph, 0, n)
                        pe.wait_ge(drain_a, ph.a0 + n - 1)
                    slot, bank = (ph.u0 + n) % 2, B[(ph.u0 + n) % 2]
                    a = wh[:, slot, k * P:(k + 1) * P]
                    nc.tensor.matmul(bank[:], a, uh[:, k, :], start=(k == 0), stop=False)
                    nc.tensor.matmul(bank[:], a, ul[:, k, :], start=False, stop=False)
                    mm = nc.tensor.matmul(bank[:], wl[:, slot, k * P:(k + 1) * P], uh[:, k, :], start=False,
                                          stop=(k == KT - 1))
                    if k == KT - 1:
                        mm.then_inc(unit_done, 1)

            for h in range(HEADS1):
                q, k, v = p1[:, h, :], p1[:, 4 + h, :], p1[:, 8 + h, :]
                if h:
                    pe.wait_ge(g_s, 3 * h)
                for c in range(NT):
                    mm = nc.tensor.transpose(B[3][:, c * P:(c + 1) * P], v[:, c * P:(c + 1) * P], ident[:])
                mm.then_inc(g_turn, 1)
                for lv in range(8):
                    n = 8 * h + lv
                    if n >= 4:
                        pe.wait_ge(g_a, n - 3)
                    if lv < 7:
                        pe.wait_ge(g_qk, 2 * (7 * h + lv) + 2)
                    else:
                        pe.wait_ge(g_k, h + 1)
                    lhs, rhs = (kl[:, lv % 2], ql[:, lv % 2]) if lv < 7 else (k, q)
                    for c in range(NT):
                        cc = slice(c * P, (c + 1) * P)
                        mm = nc.tensor.matmul(B[4 + n % 4][:, cc], lhs[:, cc], rhs[:, cc], start=True, stop=True)
                    mm.then_inc(g_p, 1)
                    a1_slot(n)
                    if n in MOD_AT:
                        pe.wait_ge(g_turned, 2 * h + 1)
                        mod_matmuls(MOD_AT[n], B[3])
                pe.wait_ge(g_kh, h + 1)
                pe.wait_ge(g_turned, 2 * h + 1)
                pe.wait_ge(mod_out, max([MOD_AT[x] + 1 for x in MOD_AT if x < 8 * h + 8]))
                for c in range(NT):
                    mm = nc.tensor.transpose(B[3][:, c * P:(c + 1) * P], kl[:, 1, c * P:(c + 1) * P], ident[:])
                mm.then_inc(g_turn, 1)
                pe.wait_ge(g_turned, 2 * h + 2)
                for c in range(3):
                    cc = slice(c * P, (c + 1) * P)
                    mm = nc.tensor.matmul(B[3][:, cc], kht[:, cc], vtm[:, cc], start=True, stop=True)
                mm.then_inc(g_u, 1)
                pe.wait_ge(g_a, 8 * (h + 1))
                pe.wait_ge(g_q0, h + 1)
                if h:
                    pe.wait_ge(ss_ok, 4 * h)
                for c in range(NT):
                    cc = slice(c * P, (c + 1) * P)
                    mm = nc.tensor.matmul(B[2][:, cc], am[:, cc], vtm[:, cc], start=True, stop=(c == 0))
                    if c:
                        pe.wait_ge(g_s, 3 * h + c)
                        mm = nc.tensor.matmul(B[2][:, cc], q0[:, cc], st[:, c - 1, :], start=False, stop=True)
                mm.then_inc(g_o, 1)

            def scores(n, i, q, k):
                nc.tensor.matmul(B[4 + i][:, 0:ZLEN[i]], q[:, i * P:(i + 1) * P], k[:, 0:ZLEN[i]],
                                 start=True, stop=True).then_inc(z_ok, 1)

            def turn_weights(job, i, z):
                kk = 4 * job + i
                pe.wait_ge(w_ok, kk + 1)
                if kk >= 2:
                    pe.wait_ge(wt_ok, kk - 1)
                for j in range(i + 1):
                    mm = nc.tensor.transpose(B[2 + kk % 2][:, j * P:(j + 1) * P],
                                             z[:, ZOFF[i] + j * P:ZOFF[i] + (j + 1) * P], ident[:])
                mm.then_inc(t_ok, 1)

            def map_scores(h, m):
                half = slice(64 * m, 64 * m + 64)
                for i in range(NT):
                    if 2 * h + m:
                        pe.wait_ge(zb_ok, 4 * (2 * h + m - 1) + i + 1)
                    scores(2 * h + m, i, p1[half, 16 + h, :], p1[half, 20 + h, :])

            for s in range(HEADS1 + 1):
                if s < HEADS1:
                    h = s
                    if h == 0:
                        pe.wait_ge(g_a, 32)
                        pe.wait_ge(ss_ok, 16)
                        pe.wait_ge(drain_a, PH["out1"].a0)
                    map_scores(h, 0)
                if s:
                    h = s - 1
                    for i in range(NT):
                        turn_weights(h, i, z1[:, 1])
                    if h >= 2:
                        pe.wait_ge(o_kept, h - 1)
                    for j in range(NT):
                        mm = nc.tensor.transpose(B[h % 2][:, j * P:(j + 1) * P],
                                                 p1[:, 24 + h, j * P:(j + 1) * P], ident[:])
                    mm.then_inc(v_turn, 1)
                if s < HEADS1:
                    map_scores(s, 1)
                if s:
                    h = s - 1
                    pe.wait_ge(v_turned, h + 1)
                    for i in range(NT):
                        pe.wait_ge(wt_ok, 4 * h + i + 1)
                        for j in range(i + 1):
                            mm = nc.tensor.matmul(B[h % 2][:, i * P:(i + 1) * P],
                                                  wt1[:, h % 2, j, i * P:(i + 1) * P],
                                                  vd1[:, h % 2, j * P:(j + 1) * P], start=(j == 0), stop=(j == i))
                    mm.then_inc(pv_ok, 1)

            for h in range(2 * HEADS1):
                src = p1[:, 8 + h, :] if h < HEADS1 else p1[:, 20 + h, :]
                pe.wait_ge(mx_n, h + 1)
                if h >= 2:
                    pe.wait_ge(mx_f, h - 1)
                else:
                    pe.wait_ge(wt_ok, 16)
                for j in range(NT):
                    mm = nc.tensor.transpose(B[2 + h % 2][:, j * P:(j + 1) * P], src[:, j * P:(j + 1) * P], ident[:])
                mm.then_inc(mx_t, 1)

            out_proj("out1", mixh, mixl, (mx_l, 0))
            norm(1)
            ffn("ff1", KT, H1)
            down("down1", 0)
            norm(2)
            norm(3)

            simple("qa2", uh, ul, 2 * KT)
            ph = PH["kv2"]
            for c in range(7):
                slot = take(ph, 0, c)
                pe.wait_ge(drain_a, ph.a0 + c - 1)
                passes(B[(ph.u0 + c) % 2], slot, KT, uh, ul, 0, True, True)
            def turn_tiles(tiles):
                for n in tiles:
                    if n >= 2:
                        pe.wait_ge(v2_turned, n - 1)
                    for j in range(NT):
                        src = (vswT[:, n] if n < 2 else gateT[:] if n == 2 else qkvb[:, 8 + n - 3])
                        mm = nc.tensor.transpose(B[2 + n % 2][:, j * P:(j + 1) * P], src[:, j * P:(j + 1) * P],
                                                 ident[:])
                    mm.then_inc(v2_turn, 1)

            pe.wait_ge(c_in, 64)
            pe.wait_ge(drain_a, PH["kv2"].a0 + 2)
            for n in range(2):
                for jj in range(16):
                    nc.tensor.matmul(B[4 + n][:, 0:GROUPS * NCMP].rearrange("p (g n) -> p g n", g=GROUPS),
                                     w1c[:, n, jj, :],
                                     kds[:, n, :, 2 * jj:2 * jj + CSTRIDE * (NCMP - 1) + 1:CSTRIDE],
                                     start=(jj == 0), stop=(jj == 15))
                pos = (POS_K, POS_V)[n]
                for jj in range(16):
                    mm = nc.tensor.matmul(B[6 + n][:, 0:1], w1c[:, n, jj, :], vt2[:, pos + jj:pos + jj + 1],
                                          start=(jj == 0), stop=(jj == 15))
                mm.then_inc(c_h, 1)
            simple("b2", uh, ul, part=(0, 2))
            pe.wait_ge(drain_a, PH["kv2"].a0 + 7)
            turn_tiles((0, 1, 2))
            pe.wait_ge(c_hg, 2)
            pe.wait_ge(v2_turned, 3)
            nc.tensor.matmul(B[2][:, 0:GROUPS * CPAD], w2c[:, 0:2, :].rearrange("p a d -> p (a d)"),
                             hc[:, 0].rearrange("p g n -> p (g n)"), start=True, stop=True)
            pe.wait_ge(c_hg, 3)
            for g_ in range(GROUPS):
                mm = nc.tensor.matmul(B[3][:, g_ * HD:(g_ + 1) * HD], hcr[:, g_].rearrange("p r n -> p (r n)"),
                                      w2c[:, 2, :], start=True, stop=True)
            mm.then_inc(c_kv, 1)
            simple("b2", uh, ul, part=(2, 4))
            pe.wait_ge(c_kvc, 2)
            for i in range(NT):
                for h in range(NSA_H):
                    half = slice(64 * (h % 2), 64 * (h % 2) + 64)
                    col = (i * REP + h // 2) * CPAD
                    mm = nc.tensor.matmul(B[6 + h % 2][:, col:col + CPAD], qa[half, h // 2, i * P:(i + 1) * P],
                                          kc[half, h // REP, :], start=True, stop=True)
            mm.then_inc(c_z, 1)
            simple("b2", uh, ul, part=(4, 6))
            pe.wait_ge(c_kvc, 2)
            pe.wait_ge(drain_a, PH["merge2"].a0)
            turn_tiles((3, 4, 5, 6))
            pe.wait_ge(v2_turned, 7)
            pe.wait_ge(c_e, 6)
            for g_ in range(GROUPS):
                for i in range(NT):
                    mm = nc.tensor.transpose(B[2 + g_][:, i * P:(i + 1) * P],
                                             zc[:, i, g_ * REP:(g_ + 1) * REP, :].rearrange("p r n -> p (r n)"),
                                             ident[:])
            mm.then_inc(c_t, 1)
            pe.wait_ge(c_wt, 1)

            def unit_operands(n):
                if n < 24:
                    h, br = (n - 8) // 2, (n - 8) % 2
                    half = slice(64 * (h % 2), 64 * (h % 2) + 64)
                    return qa[half, h // 2, :], kdup[half, br, h // REP, :]
                h = n - 24
                half = slice(64 * (h % 2), 64 * (h % 2) + 64)
                return qkvb[half, h // 2, :], qkvb[half, 4 + h // 2, :]

            for s in range(8, 33):
                if s < 32:
                    q, k = unit_operands(s)
                    for i in range(NT):
                        if s > 24:
                            pe.wait_ge(sb_s, 2 * (4 * (s - 25) + i + 1))
                        else:
                            pe.wait_ge(zb_ok, 4 * (s - 1) + i + 1)
                        scores(s, i, q, k)
                if s > 8:
                    n = s - 1
                    job = n - 4
                    for i in range(NT):
                        turn_weights(job, i, z2[:, n % 2] if n < 24 else z2[:, 1])
                    h = (n - 8) // 2 if n < 24 else n - 24
                    pair = h // 2 if n < 24 else 4 + h // 2
                    rows = slice(64 * (h % 2), 64 * (h % 2) + 64)
                    o = B[pair % 2]
                    if h % 2 == 0 and (n >= 24 or (n - 8) % 2 == 0) and pair >= 2:
                        pe.wait_ge(ml_ok, pair - 1)
                    if n < 24 and (n - 8) % 2 == 0:
                        r = h % REP
                        nc.tensor.matmul(o[rows, :], vc[CPAD * r:CPAD * (r + 1), h // REP, :],
                                         wct[CPAD * r:CPAD * (r + 1), h // REP, :], start=True, stop=False)
                    pe.wait_ge(wt_ok, 4 * (job + 1))
                    for j in range(NT):
                        if n < 24:
                            v = vsw[:, (n - 8) % 2, j * P + HD * (h // REP):j * P + HD * (h // REP) + HD]
                        else:
                            v = vbt[:, h // 2, j * P + HD * (h % 2):j * P + HD * (h % 2) + HD]
                        last = j == NT - 1 and (n >= 24 or (n - 8) % 2 == 1)
                        mm = nc.tensor.matmul(o[rows, j * P:T], v, wt2[:, j, j * P:T],
                                              start=(n >= 24 and j == 0), stop=last)
                    mm.then_inc(pv_ok, 1)

            pe.wait_ge(ml_ok, 8)
            ph = PH["merge2"]
            with pe.Fori(0, ph.iters) as i:
                for c in range(4):
                    slot = take(ph, i, c)
                    if c < 2:
                        pe.wait_ge(drain_a, i * 2 + (ph.a0 + c))
                        passes(B[c], slot, KT, uh, ul, 0, True, True)
                    else:
                        pe.wait_ge(drain_v, i * 2 + ph.d0)
                        passes(B[c], slot, 4, mih, mil, 4 * (c - 2), True, True)
            out_proj("out2", yh, yl, (y_l, 0))
            norm(4)
            ffn("ff2", 3 * KT, H1 + FT)
            down("down2", FT)
            norm(5)
            for k in range(KT):
                pe.wait_ge(o_n, k + 1)
                if k >= 2:
                    pe.wait_ge(o_c, k - 1)
                for j in range(NT):
                    mm = nc.tensor.transpose(B[k % 2][:, j * P:(j + 1) * P], onorm[:, k % 2, j * P:(j + 1) * P],
                                             ident[:])
                mm.then_inc(o_t, 1)

        @block.scalar
        def _(act):
            A = nc.scalar.activation

            def square_res(k, t, tile):
                if not (isinstance(t, int) and k == 0 and t < 2):
                    act.wait_ge(ssq_ok, t + (9 * k))

            def norm_std(k):
                act.wait_ge(n_sum, k + 1)
                A(sq[:, 0], B[4][:], ACT.Sqrt, bias=epst, scale=1.0 / D).then_inc(n_std, 1)

            def norm_u(k, nu, shift):
                act.wait_ge(gain_ok, nu + 1)
                for t in range(KT):
                    c = t % 2
                    act.wait_ge(n_t, KT * nu + t + 1)
                    if KT * nu + t >= 2:
                        act.wait_ge(n_ul, KT * nu + t - 1)
                    A(u32[:, c], tn[:, c], ACT.Identity, bias=shift[:, t:t + 1],
                      scale=gain[:, nu, t:t + 1]).then_inc(n_u32, 1)
                    A(uh[:, t, :], tn[:, c], ACT.Identity, bias=shift[:, t:t + 1],
                      scale=gain[:, nu, t:t + 1]).then_inc(n_uh, 1)

            def mod_drain(m, chunk, step, bank=B[5]):
                modt, vt = (mod1, vt1) if m == 0 else (mod2, vt2)
                act.wait_ge(mod_sum, step + 1)
                A(modt[:, ds(chunk * 2, 1)], bank[:, 0:1], ACT.Identity, bias=vt[:, ds(chunk * 2, 1)])
                A(modt[:, ds(chunk * 2 + 1, 1)], bank[:, 1:2], ACT.Identity,
                  bias=vt[:, ds(chunk * 2 + 1, 1)]).then_inc(mod_out, 1)

            def drain(name, dst, col0, func, part=None):
                ph = PH[name]

                def body(i, m, chunk):
                    for c in range(2):
                        act.wait_ge(unit_done, i * 2 + (ph.u0 + c + 1) + U1)
                        A(dst[:, ds(i * 2 + (col0 + c), 1), :].rearrange("p a t -> p (a t)"),
                          B[(ph.u0 + c) % 2][:], func).then_inc(drain_a, 1)
                    if m is not None:
                        mod_drain(m, chunk, i + MOD0[name])
                over(act, name, body, part=part)

            def residual_squares(name, k):
                ph = PH[name]

                def body(i, m, chunk):
                    for c in range(2):
                        act.wait_ge(drain_v, i * 2 + (ph.d0 + c + 1))
                        act.wait_ge(ssq_ok, i * 2 + (9 * k + c))
                        A(sq[:, c], res[:, ds(i * 2 + c, 1), :].rearrange("p a t -> p (a t)"),
                          ACT.Square).then_inc(sq_ok, 1)
                    if m is not None:
                        mod_drain(m, chunk, i + MOD0[name])
                over(act, name, body)

            def ffn(name, base):
                ph = PH[name]

                def body(i, m, chunk):
                    act.wait_ge(unit_done, i * 2 + (ph.u0 + 1) + U1)
                    A(sg[:, 0], B[0][:], ACT.Silu).then_inc(drain_a, 1)
                    act.wait_ge(h_ok, i + (base + H1 + 1))
                    A(hh[:, ds(i, 1), :].rearrange("p a t -> p (a t)"), hf[:, 0], ACT.Copy).then_inc(hh_ok, 1)
                    if m is not None:
                        mod_drain(m, chunk, i + MOD0[name])
                over(act, name, body)

            act.wait_ge(zeroed, 2)
            row = lambda name, k: t_in[name].rearrange("o (k p) -> (o k) p", p=P)
            loads = [(v1, B_ADA, "b_ada", 48), (v1, NORM_A, "norm1_w", 8), (v1, NORM_B, "norm2_w", 8),
                     (v1, LB, "hgrn_lb_logits", 8), (v1, GNORM, "hgrn_gnorm_w", 1), (v1, SUBLN, "diff_subln_w", 1),
                     (v2, B_ADA, "b_ada_2", 48), (v2, NORM_A, "norm_mix_g_2", 8), (v2, NORM_B, "norm_ffn_g_2", 8)]
            for v, r, name, k in loads:
                act.dma_start(v[r:r + k, :], row(name, k)).then_inc(vec_in, 16)
            for v, name in ((v1, "final_norm_w"), (v2, "norm_final_g_2")):
                act.dma_start(v[NORM_F:NORM_F + 8, :], t_in[name].rearrange("(k p) -> k p", p=P)).then_inc(vec_in, 16)
            for r, name in ((POS_K, "cmp_pos_k_2"), (POS_V, "cmp_pos_v_2")):
                act.dma_start(v2[r:r + 16, :], t_in[name][0].rearrange("(j a) d -> j (a d)", a=2)).then_inc(vec_in, 16)
            for k, name in enumerate(("diff_lambda_q1", "diff_lambda_k1", "diff_lambda_q2", "diff_lambda_k2")):
                act.dma_start(lamv[:, k, :], t_in[name].broadcast_to([P, HD])).then_inc(vec_in, 16)
            act.wait_ge(ct_in, 32)
            A(sc_c[:], ct[:], ACT.Silu).then_inc(setup_a, 1)
            for k in range(KT):
                act.wait_ge(x_turned, k + 1)
                A(res[:, k, :], B[k % 2][:], ACT.Copy).then_inc(drain_a, 1)
                act.wait_ge(drain_a, k + 1)
                if k >= 2:
                    act.wait_ge(ssq_ok, k)
                A(sq[:, k % 2], res[:, k, :], ACT.Square).then_inc(sq_ok, 1)
            norm_std(0)
            act.wait_ge(vecT, 1)
            A(vt1[:], B[6][:, 0:P], ACT.Copy)
            A(vt2[:], B[6][:, P:2 * P], ACT.Copy).then_inc(vecT_out, 1)
            norm_u(0, 0, mod1[:, 0:8])
            act.wait_ge(setup_v, 5)
            A(lsc[:, 4:12], lsc[:, 4:12], ACT.Exp)
            A(lsc[:, 20:22], lsc[:, 20:22], ACT.Exp).then_inc(setup_a, 1)
            drain("q1", p1, 0, ACT.Copy)
            drain("f1", p1, 4, ACT.Sigmoid)
            drain("i1", p1, 8, ACT.Copy)
            drain("g1", p1, 12, ACT.Silu)

            def a1_drain(n):
                ph = PH["a1"]
                act.wait_ge(unit_done, ph.u0 + n + 1 + U1)
                A(p1[:, 16 + n, :], B[(ph.u0 + n) % 2][:], ACT.Copy).then_inc(drain_a, 1)

            def log_decay(h):
                act.wait_ge(g_k, h + 1)
                A(ff[:], ff[:], ACT.Ln).then_inc(g_ln, 1)

            def exp_level(h, lv):
                act.wait_ge(g_x, 9 * h + lv + 1)
                src, dst = (bb[:], xx[:, 1]) if lv == 7 else (xx[:, lv % 2], xx[:, lv % 2])
                A(dst, src, ACT.Exp).then_inc(g_e, 1)

            def drains_of_slot(p):
                if p in DRAIN_AT:
                    a1_drain(DRAIN_AT[p])
                if p in MOD_AT:
                    mod_drain(0, MOD_AT[p], MOD_AT[p], B[3])

            log_decay(0)
            exp_level(0, 0)
            for h in range(HEADS1):
                act.wait_ge(g_turn, 2 * h + 1)
                A(vtm[:], B[3][:], ACT.Copy).then_inc(g_turned, 1)
                for lv in range(1, 8):
                    exp_level(h, lv)
                    drains_of_slot(8 * h + lv - 1)
                drains_of_slot(8 * h + 7)
                exp_level(h, 8)
                if h + 1 < HEADS1:
                    log_decay(h + 1)
                act.wait_ge(g_turn, 2 * h + 2)
                A(kht[:], B[3][:], ACT.Copy).then_inc(g_turned, 1)
                if h + 1 < HEADS1:
                    exp_level(h + 1, 0)
                act.wait_ge(g_o, h + 1)
                A(p1[:, 8 + h, :], B[2][:], ACT.Copy)
                for c in range(NT):
                    if h or c:
                        act.wait_ge(ss_ok, 4 * h + c)
                    mm = A(junk[:, 0:P], B[2][:, c * P:(c + 1) * P], ACT.Square,
                           scale=SQ_SCALE, accum_out=ssh[:, 4 * h + c:4 * h + c + 1])
                    mm.then_inc(ss_ok, 1)
            a1_drain(A1_UNITS - 1)

            def exps(n, i, z):
                act.wait_ge(m_ok, 4 * n + i + 1)
                c = 4 * (n % 2) + i
                sl = z[:, ZOFF[i]:ZOFF[i] + ZLEN[i]]
                A(sl, sl, ACT.Exp, bias=nmx[:, c:c + 1], scale=SCALE,
                  accum_out=sums[:, c:c + 1]).then_inc(e_ok, 1)

            def take_turned(job, i, wt):
                kk = 4 * job + i
                act.wait_ge(t_ok, kk + 1)
                A(wt[:, 0:i + 1, i * P:(i + 1) * P],
                  B[2 + kk % 2][:, 0:ZLEN[i]].rearrange("p (j t) -> p j t", j=i + 1), ACT.Copy).then_inc(wt_ok, 1)

            def output_squares(h):
                act.wait_ge(o_clamped, h + 1)
                for c in range(NT):
                    act.wait_ge(ss_ok, 16 + 4 * h + c)
                    A(junk1[:, 0:P], clamped[:, c * P:(c + 1) * P], ACT.Square, scale=SQ_SCALE,
                      accum_out=ssh[:, 16 + 4 * h + c:17 + 4 * h + c]).then_inc(ss_ok, 1)

            for s in range(HEADS1 + 1):
                if s >= 3:
                    act.wait_ge(pv_ok, s - 2)
                if s:
                    h = s - 1
                    for i in range(NT):
                        take_turned(h, i, wt1[:, h % 2])
                    act.wait_ge(v_turn, h + 1)
                    A(vd1[:, h % 2], B[h % 2][:], ACT.Copy).then_inc(v_turned, 1)
                if s >= 2:
                    output_squares(s - 2)
                if s < HEADS1:
                    for m in range(2):
                        for i in range(NT):
                            exps(2 * s + m, i, z1[:, m])
                if s:
                    act.wait_ge(pv_ok, s)
                    A(p1[:, 23 + s, :], B[(s - 1) % 2][:], ACT.Copy).then_inc(o_kept, 1)
            output_squares(HEADS1 - 1)
            act.wait_ge(rs_ok, 2)
            A(rsh, ssh, ACT.Sqrt, bias=epst, scale=SQ_BACK / P).then_inc(rs_ok, 1)
            for h in range(2 * HEADS1):
                act.wait_ge(mx_f, h + 1)
                A(mixh[:, h, :], z1[:, h % 2, 0:T], ACT.Copy).then_inc(mx_h, 1)

            act.wait_ge(mx_l, KT)
            residual_squares("out1", 1)
            norm_std(1)
            norm_u(1, 1, mod1[:, 24:32])
            ffn("ff1", 0)
            residual_squares("down1", 2)
            norm_std(2)
            for t in range(KT):
                act.wait_ge(n_res, t + 1)
                act.wait_ge(ssq_ok, 9 * 3 + t)
                A(sq[:, t % 2], res[:, t, :], ACT.Square).then_inc(sq_ok, 1)
            norm_std(3)
            norm_u(3, 2, mod2[:, 0:8])

            drain("qa2", qa, 0, ACT.Copy)
            ph = PH["kv2"]
            for c in range(7):
                bank = B[(ph.u0 + c) % 2]
                act.wait_ge(unit_done, ph.u0 + c + 1 + U1)
                if c < 2:
                    for g_ in range(GROUPS):
                        A(kds[0:64, c, g_, :], bank[64 * g_:64 * g_ + 64, :], ACT.Copy)
                        mm = A(kds[64:128, c, g_, 0:T - 1], bank[64 * g_:64 * g_ + 64, 1:T], ACT.Copy)
                elif c in (2, 4):
                    for g_ in range(GROUPS):
                        for half in range(2):
                            mm = A(kdup[64 * half:64 * half + 64, c // 2 - 1, g_, :],
                                   bank[64 * g_:64 * g_ + 64, :], ACT.Copy)
                elif c in (3, 5):
                    mm = A(vswT[:, c // 2 - 1, :], bank[:], ACT.Copy)
                else:
                    mm = A(gateT[:], bank[:], ACT.Sigmoid)
                mm.then_inc(drain_a, 1)
            for n in range(2):
                act.wait_ge(c_hx, n + 1)
                A(hc[:, n, :, 0:NCMP], hx[:, n].rearrange("p (g n) -> p g n", g=GROUPS),
                  ACT.Gelu_apprx_tanh).then_inc(c_hg, 1)
            act.wait_ge(c_hg, 2)
            for r in range(REP):
                mm = A(hcr[:, :, r, :], hc[:, 1], ACT.Copy)
            mm.then_inc(c_hg, 1)

            def take_tiles(tiles):
                for n in tiles:
                    act.wait_ge(v2_turn, n + 1)
                    bank = B[2 + n % 2]
                    if n == 2:
                        mm = A(gt[:], bank[:].rearrange("p (i c) -> p i c", i=NT)[:, :, 0:24], ACT.Copy)
                    else:
                        mm = A(vsw[:, n] if n < 2 else vbt[:, n - 3], bank[:], ACT.Copy)
                    mm.then_inc(v2_turned, 1)

            drain("b2", qkvb, 0, ACT.Copy, part=(0, 2))
            take_tiles((0, 1, 2))
            act.wait_ge(c_kv, 1)
            A(kc[:], B[2][:, 0:GROUPS * CPAD].rearrange("p (g n) -> p g n", g=GROUPS), ACT.Copy).then_inc(c_kvc, 1)
            A(vc[:], B[3][:, 0:P].rearrange("p (g d) -> p g d", g=GROUPS), ACT.Copy).then_inc(c_kvc, 1)
            drain("b2", qkvb, 0, ACT.Copy, part=(2, 4))
            act.wait_ge(c_v, 4)
            zcf = zc[:].rearrange("p i h n -> p (i h n)")
            A(zcf, zcf, ACT.Exp, scale=SCALE).then_inc(c_e, 1)
            drain("b2", qkvb, 0, ACT.Copy, part=(4, 6))
            act.wait_ge(tab2, N_TAB2)
            take_tiles((3, 4, 5, 6))
            act.wait_ge(c_t, 1)
            A(wct[:, 0], B[2][:], ACT.Copy)
            A(wct[:, 1], B[3][:], ACT.Copy).then_inc(c_wt, 1)

            def take_pair(n):
                pair = (n - 8) // 4 if n < 24 else 4 + (n - 24) // 2
                if (n < 24 and (n - 8) % 4 == 3) or (n >= 24 and n % 2 == 1):
                    act.wait_ge(pv_ok, n - 3)
                    A(mih[:, pair, :], B[pair % 2][:], ACT.Copy).then_inc(mh_ok, 1)

            for s in range(8, 33):
                if s > 8:
                    act.wait_ge(pv_ok, s - 1 - 4)
                for step in range(NT + 1):
                    if s > 8 and step < NT:
                        take_turned(s - 1 - 4, step, wt2)
                    for i in ([] if step == 0 else [step - 1]):
                        if s < 24:
                            exps(s, i, z2[:, s % 2])
                        elif s < 32:
                            k = 4 * (s - 24) + i
                            act.wait_ge(sb_m, k + 1)
                            sl = slice(ZOFF[i], ZOFF[i] + ZLEN[i])
                            A(z2[:, 0, sl], B[4 + i][:, 0:ZLEN[i]], ACT.Sigmoid, scale=-SCALE).then_inc(sb_s, 1)
                            A(z2[:, 1, sl], B[4 + i][:, 0:ZLEN[i]], ACT.Sigmoid, scale=SCALE).then_inc(sb_s, 1)
                if s > 8:
                    take_pair(s - 1)

            act.wait_ge(ml_ok, 8)
            ph = PH["merge2"]
            with act.Fori(0, ph.iters) as i:
                for c in range(2):
                    act.wait_ge(unit_done, i * 4 + (ph.u0 + c + 1) + U1)
                    act.wait_ge(y_f, i + Y1)
                    A(ms[:, c], B[c][:], ACT.Sigmoid).then_inc(drain_a, 1)
                act.wait_ge(y_f, i + (Y1 + 1))
                A(yh[:, ds(i, 1), :].rearrange("p a t -> p (a t)"), yf[:, 0], ACT.Copy).then_inc(y_h, 1)
            residual_squares("out2", 4)
            norm_std(4)
            norm_u(4, 3, mod2[:, 24:32])
            ffn("ff2", FT)
            residual_squares("down2", 5)
            norm_std(5)
            for k in range(KT):
                act.wait_ge(o_t, k + 1)
                A(outb[:, :, k * P:(k + 1) * P], B[k % 2][:].rearrange("p (j f) -> p j f", j=NT),
                  ACT.Copy).then_inc(o_c, 1)

        @block.vector
        def _(v):
            V = nc.vector
            seq = [0]

            def split(u, slot, landed=None, nk=KT):
                first = isinstance(u, int) and u < 2
                v.wait_ge(w_in[slot], 16 * (u // 2 + 1) if landed is None else landed)
                if not first:
                    v.wait_ge(unit_done, u - 1 + U1)
                n = nk * P
                V.tensor_copy(wh[:, slot, 0:n], wraw[:, slot, 0:n]).then_inc(w_hi, 1)
                v.wait_ge(w_hi, u + 1)
                V.tensor_tensor(wl[:, slot, 0:n], wraw[:, slot, 0:n], wh[:, slot, 0:n].bitcast(F32),
                                ALU.subtract).then_inc(w_split, 1)

            def ahead(ph, i, c, nk=KT):
                uc = ph.u0 + c + 1
                landed = None if isinstance(i, int) else i * (8 * ph.units) + 16 * (uc // 2 + 1)
                split(i * ph.units + uc, uc % 2, landed, nk)

            def mod_products(step):
                for k in range(KT):
                    src, scale = ada0[:, step, k, :], sc_c[:, 0, k:k + 1]
                    if k == 0:
                        ins = V.tensor_scalar(acc0[:, step], src, scale, None, ALU.mult)
                    else:
                        v.wait_ge(mod_step, step * (KT - 1) + k)
                        ins = V.scalar_tensor_tensor(acc0[:, step], src, scale, acc0[:, step],
                                                     op0=ALU.mult, op1=ALU.add)
                    if k < KT - 1:
                        ins.then_inc(mod_step, 1)
                    else:
                        ins.then_inc(mod_acc, 1 if step < V_CHUNKS - 1 else 8 - step)

            def loop(ph, body, part=None):
                a, b = part or (0, ph.iters)
                with v.Fori(a, b) as i:
                    body(i)

            def plain(name, part=None):
                ph = PH[name]

                def body(i):
                    for c in range(ph.units):
                        ahead(ph, i, c)
                loop(ph, body, part)

            def add_residual(name, gates, skip_last=False):
                ph = PH[name]
                per = ph.units // 2

                def body(i, last=False):
                    for t in range(2):
                        for c in range(per):
                            if not (last and t == 1 and c == per - 1):
                                ahead(ph, i, t * per + c)
                        v.wait_ge(unit_done, i * ph.units + (ph.u0 + (t + 1) * per) + U1)
                        if isinstance(i, int):
                            r, gcol = res[:, 2 * i + t, :], gates[:, 2 * i + t:2 * i + t + 1]
                        else:
                            r = res[:, ds(i * 2 + t, 1), :].rearrange("p a t -> p (a t)")
                            gcol = gates[:, ds(i * 2 + t, 1)]
                        V.scalar_tensor_tensor(r, B[t][:], gcol, r, op0=ALU.mult, op1=ALU.add).then_inc(drain_v, 1)
                if not skip_last:
                    loop(ph, body)
                else:
                    with v.Fori(0, ph.iters - 1) as i:
                        body(i)
                    body(ph.iters - 1, last=True)

            def norm_rstd(k):
                v.wait_ge(n_std, k + 1)
                V.reciprocal(rstd[:], sq[:, 0]).then_inc(n_rstd, 1)
                v.wait_ge(n_rstd, k + 1)

            def norm_u(nu):
                for t in range(KT + 1):
                    if t < KT:
                        if KT * nu + t >= 2:
                            v.wait_ge(n_uh, KT * nu + t - 1)
                        V.tensor_tensor(tn[:, t % 2], res[:, t, :], rstd[:], ALU.mult).then_inc(n_t, 1)
                    if t:
                        s = t - 1
                        v.wait_ge(n_uh, KT * nu + s + 1)
                        V.tensor_tensor(ul[:, s, :], u32[:, s % 2], uh[:, s, :].bitcast(F32),
                                        ALU.subtract).then_inc(n_ul, 1)

            def gains(nu, modt, vt, norm_row, sc_col):
                V.scalar_tensor_tensor(gain[:, nu, :], modt[:, sc_col:sc_col + 8], 1.0,
                                       vt[:, norm_row:norm_row + 8], op0=ALU.add, op1=ALU.mult).then_inc(gain_ok, 1)

            def ffn(name, base):
                ph = PH[name]

                def body(i):
                    ahead(ph, i, 0)
                    ahead(ph, i, 1)
                    v.wait_ge(unit_done, i * 2 + (ph.u0 + 2) + U1)
                    v.wait_ge(drain_a, i + (ph.a0 + 1))
                    V.tensor_tensor(hf[:, 0], sg[:, 0], B[1][:], ALU.mult).then_inc(h_ok, 1)
                    v.wait_ge(hh_ok, i + (base + 1))
                    V.tensor_tensor(hl[:, ds(i, 1), :].rearrange("p a t -> p (a t)"), hf[:, 0],
                                    hh[:, ds(i, 1), :].rearrange("p a t -> p (a t)").bitcast(F32),
                                    ALU.subtract).then_inc(hl_ok, 1)
                loop(ph, body)

            sv = [0]

            def link(ins):
                ins.then_inc(setup_v, 1)
                sv[0] += 1
                v.wait_ge(setup_v, sv[0])

            V.memset(tiny[:, 45:46], 0.0).then_inc(drain_v, 2)
            V.memset(tiny[:, 46:47], 0.0).then_inc(h_ok, H1)
            V.memset(tiny[:, 47:48], 0.0).then_inc(y_f, Y1)
            v.wait_ge(setup_a, 1)
            for s in range(V_CHUNKS):
                v.wait_ge(ada0_in[s], 16)
                mod_products(s)
            norm_rstd(0)
            v.wait_ge(vecT_out, 1)
            l0, l1 = vt1[:, LB:LB + 4], vt1[:, LB + 4:LB + 8]
            link(V.tensor_tensor(lsc[:, 0:4], l0, l1, ALU.max))
            link(V.tensor_tensor(lsc[:, 4:8], l0, lsc[:, 0:4], ALU.subtract))
            link(V.tensor_tensor(lsc[:, 8:12], l1, lsc[:, 0:4], ALU.subtract))
            for m in range(2):
                link(V.tensor_tensor_reduce(lamv[:, 2 * m, :], lamv[:, 2 * m, :], lamv[:, 2 * m + 1, :], 1.0, 0.0,
                                            ALU.mult, ALU.add, lsc[:, 20 + m:21 + m]))
            v.wait_ge(mod_sum, 8)
            V.tensor_tensor(mod1[:, 0:16], B[5][:, 0:16], vt1[:, 0:16], ALU.add).then_inc(mod_out, 8)
            v.wait_ge(mod_out, 8)
            gains(0, mod1, vt1, NORM_A, 8)
            split(0, 0)
            norm_u(0)
            v.wait_ge(setup_a, 2)
            link(V.tensor_tensor(lsc[:, 12:16], lsc[:, 4:8], lsc[:, 8:12], ALU.add))
            link(V.reciprocal(lsc[:, 16:20], lsc[:, 12:16]))
            link(V.tensor_tensor(lbs, lsc[:, 4:8], lsc[:, 16:20], ALU.mult))
            link(V.tensor_scalar(oml, lbs, -1.0, 1.0, ALU.mult, ALU.add))
            link(V.tensor_tensor(lsc[:, 22:23], lsc[:, 20:21], lsc[:, 21:22], ALU.subtract))
            link(V.tensor_scalar(nlam, lsc[:, 22:23], LAMBDA_INIT, -1.0, ALU.add, ALU.mult))
            plain("q1")
            plain("f1")
            v.wait_ge(const_ok, 4 + 4)
            mk = [0]

            def mlink(ins):
                ins.then_inc(g_zero, 1)
                mk[0] += 1
                v.wait_ge(g_zero, mk[0])

            S_, T_ = lmask[:, 6, :], lmask[:, 7, :]
            gtm, xor, ge, lt = (scrap[:, n, :] for n in range(4))
            mlink(V.tensor_tensor(gtm, T_, S_, ALU.is_gt))
            mlink(V.tensor_tensor(xor, T_, S_, ALU.bitwise_xor))
            mlink(V.tensor_scalar(lmask[:, 7, :], xor, 0.0, None, ALU.is_equal))

            def level_masks(levels):
                for lv in levels:
                    m = LEVELS[lv]
                    mlink(V.tensor_scalar(ge, xor, float(m), None, ALU.is_ge))
                    mlink(V.tensor_scalar(lt, xor, float(2 * m), None, ALU.is_lt))
                    mlink(V.tensor_tensor(ge, ge, lt, ALU.mult))
                    mlink(V.tensor_tensor(lmask[:, lv, :], ge, gtm, ALU.mult))

            level_masks((0, 1))
            plain("i1")
            level_masks((2, 3, 4))
            plain("g1")
            level_masks((5, 6))


            def split_next(n):
                u = PH["a1"].u0 + n + 1
                split(u, u % 2)

            def forget(h):
                fk = p1[:, 4 + h, :]
                V.tensor_scalar(ff[:], fk, oml[:, h:h + 1], lbs[:, h:h + 1], ALU.mult, ALU.add).then_inc(g_f, 1)
                v.wait_ge(g_f, h + 1)
                V.tensor_scalar(fk, ff[:], -1.0, 1.0, ALU.mult, ALU.add).then_inc(g_k, 1)

            def decay_sums(h):
                v.wait_ge(g_ln, h + 1)
                V.tensor_tensor_scan(bb[:], rmask[:], ff[:], 0.0, ALU.mult, ALU.add).then_inc(g_bb, 1)
                v.wait_ge(g_bb, h + 1)

            def exponents(lv):
                m = LEVELS[lv]
                bv = bb[:].rearrange("p (n c) -> p n c", c=2 * m)
                xv = xx[:, lv % 2].rearrange("p (n c) -> p n c", c=2 * m)
                ref = bv[:, :, m - 1:m].broadcast_to([P, T // (2 * m), m])
                V.tensor_tensor(xv[:, :, m:2 * m], bv[:, :, m:2 * m], ref, ALU.subtract)
                V.tensor_tensor(xv[:, :, 0:m], ref, bv[:, :, 0:m], ALU.subtract).then_inc(g_x, 1)

            v.wait_ge(drain_a, PH["a1"].a0)
            forget(0)
            decay_sums(0)
            exponents(0)
            for h in range(HEADS1):
                q, fk = p1[:, h, :], p1[:, 4 + h, :]

                def products(lv):
                    m = LEVELS[lv]
                    n = 7 * h + lv
                    v.wait_ge(g_e, 9 * h + lv + 1)
                    if n >= 2:
                        v.wait_ge(g_p, 8 * h + lv - 1 if lv >= 2 else 8 * (h - 1) + 8)
                    if h and lv < 2:
                        v.wait_ge(g_turn, 2 * h)
                    ev = xx[:, lv % 2].rearrange("p (n c) -> p n c", c=2 * m)
                    for dst, src, a in ((ql, q, m), (kl, fk, 0)):
                        dv = dst[:, lv % 2].rearrange("p (n c) -> p n c", c=2 * m)
                        sv_ = src.rearrange("p (n c) -> p n c", c=2 * m)
                        V.tensor_tensor(dv[:, :, a:a + m], sv_[:, :, a:a + m], ev[:, :, a:a + m],
                                        ALU.mult).then_inc(g_qk, 1)

                def merge(lv):
                    n = 8 * h + lv
                    v.wait_ge(g_p, n + 1)
                    if n:
                        v.wait_ge(g_a, n)
                    if h and lv == 0:
                        v.wait_ge(g_o, h)
                    V.copy_predicated(am[:].rearrange("p (c t) -> p c t", c=NT),
                                      lmask[:, lv, :].unsqueeze(1).broadcast_to([P, NT, P]),
                                      B[4 + n % 4][:].rearrange("p (c t) -> p c t", c=NT)).then_inc(g_a, 1)

                if h == 0:
                    v.wait_ge(g_cleared, 3)
                for lv in range(7):
                    if lv + 1 < 7:
                        if lv:
                            v.wait_ge(g_qk, 2 * (7 * h + lv))
                        elif h:
                            v.wait_ge(g_s, 3 * h)
                        exponents(lv + 1)
                    products(lv)
                    if lv:
                        merge(lv - 1)
                    if 8 * h + lv in SPLIT_AT:
                        split_next(SPLIT_AT[8 * h + lv])
                if h + 1 < HEADS1:
                    forget(h + 1)
                v.wait_ge(g_qk, 14 * (h + 1))
                V.tensor_tensor(xx[:, 0].rearrange("p (c t) -> p c t", c=NT),
                                bb[:].rearrange("p (c t) -> p c t", c=NT)[:, :, P - 1:P].broadcast_to([P, NT, P]),
                                bb[:].rearrange("p (c t) -> p c t", c=NT), ALU.subtract).then_inc(g_x, 2)
                merge(6)
                v.wait_ge(g_e, 9 * h + 8)
                if h:
                    v.wait_ge(g_o, h)
                V.tensor_tensor(q0[:], q, xx[:, 1], ALU.mult).then_inc(g_q0, 1)
                v.wait_ge(g_e, 9 * h + 9)
                v.wait_ge(g_p, 8 * h + 8)
                V.tensor_tensor(kl[:, 1], fk, xx[:, 0], ALU.mult).then_inc(g_kh, 1)
                merge(7)
                if 8 * h + 7 in SPLIT_AT:
                    split_next(SPLIT_AT[8 * h + 7])
                if h + 1 < HEADS1:
                    v.wait_ge(g_kh, h + 1)
                    decay_sums(h + 1)
                    exponents(0)
                v.wait_ge(g_u, h + 1)
                if h:
                    v.wait_ge(g_o, h)
                V.tensor_copy(st[:, 0, :], B[3][:, 0:P]).then_inc(g_s, 1)
                for c in (1, 2):
                    v.wait_ge(g_s, 3 * h + c)
                    V.scalar_tensor_tensor(st[:, c, :], st[:, c - 1, :], xx[:, 1, c * P + P - 1:c * P + P],
                                           B[3][:, c * P:(c + 1) * P], op0=ALU.mult, op1=ALU.add).then_inc(g_s, 1)

            def biased(n, i, z, table, turned):
                v.wait_ge(z_ok, 4 * n + i + 1)
                if turned and i == 0:
                    v.wait_ge(t_ok, turned)
                c = 4 * (n % 2) + i
                if n >= 2:
                    v.wait_ge(e_ok, 4 * (n - 2) + i + 1)
                V.tensor_tensor_reduce(z[:, ZOFF[i]:ZOFF[i] + ZLEN[i]], B[4 + i][:, 0:ZLEN[i]],
                                       table[:, 384 - P * i:T], 1.0, -3.0e38, ALU.add, ALU.max,
                                       mxs[:, c:c + 1]).then_inc(zb_ok, 1)
                v.wait_ge(zb_ok, 4 * n + i + 1)
                V.tensor_scalar(nmx[:, c:c + 1], mxs[:, c:c + 1], -SCALE, None, ALU.mult).then_inc(m_ok, 1)

            dt = [0]

            def next_table(table, ratio):
                V.tensor_scalar(table[:], table[:], ratio, None, ALU.mult).then_inc(d_tab, 1)
                dt[0] += 1
                v.wait_ge(d_tab, dt[0])

            rr = [0]

            def rlink(ins):
                ins.then_inc(r_ok, 1)
                rr[0] += 1
                v.wait_ge(r_ok, rr[0])

            v.wait_ge(g_o, 4)
            v.wait_ge(const_ok, 4 + 4 + 2)
            def clamp(h):
                v.wait_ge(o_kept, h + 1)
                if h:
                    v.wait_ge(ss_ok, 16 + 4 * h)
                V.tensor_scalar(clamped[:], p1[:, 24 + h, :], CLAMP, -CLAMP, ALU.min, ALU.max).then_inc(o_clamped, 1)

            for s in range(HEADS1 + 1):
                if s:
                    v.wait_ge(e_ok, 8 * s)
                    rlink(V.reciprocal(rcs, sums))
                    rlink(V.tensor_scalar(rcs[:, 4:8], rcs[:, 4:8], nlam, None, ALU.mult))
                    maps = [[z1[:, m, ZOFF[i]:ZOFF[i] + ZLEN[i]] for m in range(2)] for i in range(NT)]
                    for i, (_, b) in enumerate(maps):
                        V.tensor_scalar(b, b, rcs[:, 4 + i:5 + i], None, ALU.mult).then_inc(r_ok, 1)
                    for i, (a, b) in enumerate(maps):
                        v.wait_ge(r_ok, rr[0] + i + 1)
                        V.scalar_tensor_tensor(b, a, rcs[:, i:i + 1], b, op0=ALU.mult, op1=ALU.add).then_inc(w_ok, 1)
                    rr[0] += NT
                    v.wait_ge(w_ok, 4 * s)
                if s >= 2:
                    clamp(s - 2)
                if s < HEADS1:
                    next_table(dm1, 0.25)
                    for i in range(NT):
                        biased(2 * s, i, z1[:, 0], dm1, 0)
                    for i in range(NT):
                        biased(2 * s + 1, i, z1[:, 1], dm1, 4 * s)
            clamp(HEADS1 - 1)
            v.wait_ge(ss_ok, 32)
            V.tensor_scalar(okh, ssh, SQ_OVER, None, ALU.is_lt).then_inc(rs_ok, 1)
            v.wait_ge(rs_ok, 1)
            V.tensor_tensor(ssh, ssh, okh, ALU.mult).then_inc(rs_ok, 1)
            v.wait_ge(rs_ok, 3)
            rlink(V.reciprocal(rsh, rsh))
            rlink(V.tensor_tensor(rsh, rsh, okh, ALU.mult))
            for h in range(2 * HEADS1):
                o = p1[:, 8 + h, :] if h < HEADS1 else p1[:, 20 + h, :]
                V.tensor_tensor(o.rearrange("p (c d) -> p c d", c=NT), o.rearrange("p (c d) -> p c d", c=NT),
                                rsh[:, 4 * h:4 * h + 4].unsqueeze(2).broadcast_to([P, NT, P]),
                                ALU.mult).then_inc(mx_n, 1)
            for h in range(2 * HEADS1 + 1):
                if h < 2 * HEADS1:
                    v.wait_ge(mx_t, h + 1)
                    if h >= 2:
                        v.wait_ge(mx_l, h - 1)
                    m = z1[:, h % 2, 0:T]
                    if h < HEADS1:
                        V.scalar_tensor_tensor(m, B[2 + h % 2][:], vt1[:, GNORM:GNORM + 1], p1[:, 12 + h, :],
                                               op0=ALU.mult, op1=ALU.mult).then_inc(mx_f, 1)
                    else:
                        V.tensor_scalar(m, B[2 + h % 2][:], vt1[:, SUBLN:SUBLN + 1], 1.0 - LAMBDA_INIT,
                                        ALU.mult, ALU.mult).then_inc(mx_f, 1)
                if h:
                    v.wait_ge(mx_h, h)
                    V.tensor_tensor(mixl[:, h - 1, :], z1[:, (h - 1) % 2, 0:T], mixh[:, h - 1, :].bitcast(F32),
                                    ALU.subtract).then_inc(mx_l, 1)

            add_residual("out1", mod1[:, 16:24])
            norm_rstd(1)
            gains(1, mod1, vt1, NORM_B, 32)
            norm_u(1)
            ffn("ff1", 0)
            add_residual("down1", mod1[:, 40:48])
            norm_rstd(2)
            for t in range(KT):
                V.scalar_tensor_tensor(res[:, t, :], res[:, t, :], vt1[:, NORM_F + t:NORM_F + t + 1], rstd[:],
                                       op0=ALU.mult, op1=ALU.mult).then_inc(n_res, 1)
            v.wait_ge(n_res, KT)
            v.wait_ge(mod_out, 48)
            gains(2, mod2, vt2, NORM_A, 8)
            norm_rstd(3)
            norm_u(2)

            plain("qa2")
            ph = PH["kv2"]
            for c in range(7):
                ahead(ph, 0, c)
            V.memset(hc[:], 0.0).then_inc(c_hb, 1)
            v.wait_ge(c_hb, 1)
            v.wait_ge(c_in, 64)
            V.tensor_copy(w2c[:, 1, :], w2c[:, 0, :]).then_inc(c_hb, 1)
            for n in range(2):
                v.wait_ge(c_h, n + 1)
                V.tensor_copy(hb[:, n:n + 1], B[6 + n][:, 0:1]).then_inc(c_hb, 1)
                v.wait_ge(c_hb, n + 3)
                V.tensor_scalar(hx[:, n], B[4 + n][:, 0:GROUPS * NCMP], hb[:, n:n + 1], None,
                                ALU.add).then_inc(c_hx, 1)
            plain("b2", (0, 2))
            plain("b2", (2, 4))
            v.wait_ge(tab2, N_TAB2)
            v.wait_ge(c_z, 1)
            z3 = zc[:].rearrange("p i h n -> p (i h) n")
            for b in range(2):
                ins = V.tensor_tensor(zc[:, :, b:NSA_H:2, :],
                                      B[6 + b][:].rearrange("p (i h n) -> p i h n", i=NT, h=REP),
                                      bc[:, :, b:NSA_H:2, :], ALU.add)
                ins.then_inc(c_v, 1)
            v.wait_ge(c_v, 2)
            V.tensor_reduce(cmx, z3, AX_X, ALU.max).then_inc(c_v, 1)
            v.wait_ge(c_v, 3)
            V.tensor_tensor(z3, z3, cmx.unsqueeze(2).broadcast_to([P, 32, CPAD]), ALU.subtract).then_inc(c_v, 1)
            plain("b2", (4, 6))
            v.wait_ge(c_e, 1)
            cl = [1]

            def clink(ins):
                ins.then_inc(c_e, 1)
                cl[0] += 1
                v.wait_ge(c_e, cl[0])
            clink(V.tensor_reduce(csm, z3, AX_X, ALU.add))
            clink(V.reciprocal(csm, csm))
            v.wait_ge(v2_turned, 3)
            clink(V.tensor_tensor(csm.rearrange("p (i h) -> p i h", i=NT), csm.rearrange("p (i h) -> p i h", i=NT),
                                  gt[:, :, 0:24:3], ALU.mult))
            clink(V.tensor_tensor(csm.rearrange("p (i h) -> p i h", i=NT), csm.rearrange("p (i h) -> p i h", i=NT),
                                  rv.unsqueeze(2).broadcast_to([P, NT, NSA_H]), ALU.mult))
            clink(V.tensor_tensor(z3, z3, csm.unsqueeze(2).broadcast_to([P, 32, CPAD]), ALU.mult))
            v.wait_ge(c_t, 1)

            for s in range(8, 33):
                if s > 8 and s - 1 < 24:
                    n = s - 1
                    h, br = (n - 8) // 2, (n - 8) % 2
                    c0 = 4 * (n % 2)
                    v.wait_ge(e_ok, 4 * (n + 1))
                    rlink(V.reciprocal(rcs[:, c0:c0 + 4], sums[:, c0:c0 + 4]))
                    rlink(V.tensor_tensor(rcs[:, c0:c0 + 4], rcs[:, c0:c0 + 4], gt[:, :, 3 * h + 1 + br], ALU.mult))
                    for i in range(NT):
                        a = z2[:, n % 2, ZOFF[i]:ZOFF[i] + ZLEN[i]]
                        V.tensor_scalar(a, a, rcs[:, c0 + i:c0 + i + 1], None, ALU.mult).then_inc(w_ok, 1)
                elif s > 24:
                    n = s - 1
                    for i in range(NT):
                        k = 4 * (n - 24) + i
                        v.wait_ge(sb_s, 2 * (k + 1))
                        if k >= 2:
                            v.wait_ge(w_ok, 4 * (n - 4) + i - 1)
                        kp = z2[:, 0, ZOFF[i]:ZOFF[i] + ZLEN[i]]
                        sgm = z2[:, 1, ZOFF[i]:ZOFF[i] + ZLEN[i] - 1]
                        r = rb[:, k % 2, 0:ZLEN[i]]
                        V.tensor_tensor_scan(r[:, ::-1], kp[:, ::-1], kp[:, ::-1], 1.0, ALU.mult,
                                             ALU.bypass).then_inc(sb_r, 1)
                        v.wait_ge(sb_r, k + 1)
                        V.tensor_tensor(sgm, sgm, r[:, 1:ZLEN[i]], ALU.mult).then_inc(w_ok, 1)
                if s < 24:
                    if s % 2 == 0:
                        if s > 8:
                            v.wait_ge(zb_ok, 4 * s)
                        next_table(dm2, 0.5)
                    for i in range(NT):
                        biased(s, i, z2[:, s % 2], dm2, 4 * (s - 2 - 4) + 4 if s >= 10 else 0)
                elif s < 32:
                    for i in range(NT):
                        k = 4 * (s - 24) + i
                        v.wait_ge(z_ok, 4 * s + i + 1)
                        zd = B[4 + i][:, i * P:(i + 1) * P]
                        V.tensor_tensor(zd, zd, nst[:], ALU.add).then_inc(sb_m, 1)
                if s > 8:
                    n = s - 1
                    pair = (n - 8) // 4 if n < 24 else 4 + (n - 24) // 2
                    if (n < 24 and (n - 8) % 4 == 3) or (n >= 24 and n % 2 == 1):
                        v.wait_ge(mh_ok, pair + 1)
                        V.tensor_tensor(mil[:, pair, :], B[pair % 2][:], mih[:, pair, :].bitcast(F32),
                                        ALU.subtract).then_inc(ml_ok, 1)

            ph = PH["merge2"]

            def y_rest(i):
                v.wait_ge(y_h, i + 1)
                sl = slice(i, i + 1) if isinstance(i, int) else ds(i, 1)
                V.tensor_tensor(yl[:, sl, :].rearrange("p a t -> p (a t)"), yf[:, 0],
                                yh[:, sl, :].rearrange("p a t -> p (a t)").bitcast(F32),
                                ALU.subtract).then_inc(y_l, 1)

            def merge_body(i, before):
                for c, nk in enumerate((KT, 4, 4, KT)):
                    ahead(ph, i, c, nk)
                    if c == 0 and before is not None:
                        y_rest(before)
                for b in range(2):
                    v.wait_ge(drain_a, i * 2 + (ph.a0 + b + 1))
                    v.wait_ge(unit_done, i * 4 + (ph.u0 + b + 3) + U1)
                    V.tensor_tensor(ms[:, b], ms[:, b], B[2 + b][:], ALU.mult).then_inc(drain_v, 1)
                v.wait_ge(drain_v, i * 2 + (ph.d0 + 2))
                V.tensor_tensor(yf[:, 0], ms[:, 0], ms[:, 1], ALU.add).then_inc(y_f, 1)

            merge_body(0, None)
            with v.Fori(0, ph.iters - 1) as i:
                merge_body(i + 1, i)
            y_rest(ph.iters - 1)
            add_residual("out2", mod2[:, 16:24])
            norm_rstd(4)
            gains(3, mod2, vt2, NORM_B, 32)
            norm_u(3)
            ffn("ff2", FT)
            add_residual("down2", mod2[:, 40:48], skip_last=True)
            norm_rstd(5)
            for k in range(KT):
                if k >= 2:
                    v.wait_ge(o_t, k - 1)
                V.scalar_tensor_tensor(onorm[:, k % 2], res[:, k, :], vt2[:, NORM_F + k:NORM_F + k + 1], rstd[:],
                                       op0=ALU.mult, op1=ALU.mult).then_inc(o_n, 1)


_INS = [
    "x", "c", "w_ada", "b_ada", "norm1_w", "w_in", "hgrn_lb_logits", "hgrn_gnorm_w", "diff_lambda_q1",
    "diff_lambda_k1", "diff_lambda_q2", "diff_lambda_k2", "diff_subln_w", "w_out", "norm2_w", "w_ffn_gate",
    "w_ffn_up", "w_ffn_down", "final_norm_w", "c_2", "w_ada_2", "b_ada_2", "norm_mix_g_2", "w_in_2",
    "cmp_pos_k_2", "cmp_w1_k_2", "cmp_w2_k_2", "cmp_pos_v_2", "cmp_w1_v_2", "cmp_w2_v_2", "w_proj_a_2",
    "w_proj_b_2", "w_out_2", "norm_ffn_g_2", "w_ffn_gate_2", "w_ffn_up_2", "w_ffn_down_2", "norm_final_g_2",
]


def kernel(**inputs):
    import numpy as _np
    import concourse.bacc as _bacc
    from concourse import mybir as _mybir
    from concourse.bass_utils import run_bass_kernel_spmd as _run

    nc = _bacc.Bacc("TRN2", target_bir_lowering=False, num_devices=1)
    arrays, t_in = {}, {}
    for name in _INS:
        a = _np.ascontiguousarray(inputs[name])
        arrays[f"in_{name}_dram"] = a
        t_in[name] = nc.dram_tensor(f"in_{name}_dram", a.shape, _mybir.dt.from_np(a.dtype), kind="ExternalInput").ap()
    out = nc.dram_tensor("out_0_dram", (1, T, D), F32, kind="ExternalOutput").ap()
    build(nc, t_in, out)
    r = _run(nc, [arrays], core_ids=[0])
    return r.results[0]["out_0_dram"]
```
